# Optimizing a Trainium2 kernel written in Bass

```python
import jax, jax.numpy as jnp
from jax import lax
import numpy as np

D_MODEL = 1024
BATCH = 1
SEQ = 512
DEPTH = 1

D_PLE = 256
N_ATTN_HEADS = 8
HEAD_DIM = 64
D_ATTN = N_ATTN_HEADS * HEAD_DIM
N_GMLP_GROUPS = 8
GMLP_GROUP_DIM = 64
D_GMLP = N_GMLP_GROUPS * GMLP_GROUP_DIM
D_MIX = D_ATTN + D_GMLP
D_IN_PROJ = 3 * D_ATTN + 2 * D_GMLP
D_FF = 4 * D_MODEL
MOBA_BLOCK = 256
MOBA_TOPK = 3
Q_CHUNK = 128
GMLP_CHUNK = 128
ROPE_THETA = 500000.0
ROPE_DIM = HEAD_DIM // 4
NORM_EPS = 1e-6
NEG_INF = -1e30

kernel_name = "hymba_moba_gmlp_hybrid_layer"

def rms_norm(x, g):
    xf = x.astype(jnp.float32)
    y = xf * lax.rsqrt(jnp.mean(xf * xf, axis=-1, keepdims=True) + NORM_EPS)
    return (y * g.astype(jnp.float32)).astype(x.dtype)

def layer_norm(x, g, b):
    xf = x.astype(jnp.float32)
    mu = jnp.mean(xf, axis=-1, keepdims=True)
    xc = xf - mu
    var = jnp.mean(xc * xc, axis=-1, keepdims=True)
    y = xc * lax.rsqrt(var + NORM_EPS) * g.astype(jnp.float32) + b.astype(jnp.float32)
    return y.astype(x.dtype)

def partial_rope(x, pos):
    half = ROPE_DIM // 2
    inv_freq = ROPE_THETA ** (-jnp.arange(half, dtype=jnp.float32) / half)
    ang = pos.astype(jnp.float32)[:, None] * inv_freq[None, :]
    cos = jnp.cos(ang)[None, :, None, :]
    sin = jnp.sin(ang)[None, :, None, :]
    xr = x[..., :ROPE_DIM].astype(jnp.float32)
    x1, x2 = xr[..., :half], xr[..., half:]
    rot = jnp.concatenate([x1 * cos - x2 * sin, x2 * cos + x1 * sin], axis=-1)
    return jnp.concatenate([rot.astype(x.dtype), x[..., ROPE_DIM:]], axis=-1)

def moba_attention(q, k, v):
    B, S, H, Dh = q.shape
    nb = -(-S // MOBA_BLOCK)
    pad = nb * MOBA_BLOCK - S
    k_p = jnp.pad(k, ((0, 0), (0, pad), (0, 0), (0, 0)))
    v_p = jnp.pad(v, ((0, 0), (0, pad), (0, 0), (0, 0)))
    k_blk = k_p.reshape(B, nb, MOBA_BLOCK, H, Dh).transpose(0, 3, 1, 2, 4)
    v_blk = v_p.reshape(B, nb, MOBA_BLOCK, H, Dh).transpose(0, 3, 1, 2, 4)

    k_mean = jnp.mean(k_blk.astype(jnp.float32), axis=3)
    pos = jnp.arange(S)
    own_blk = pos // MOBA_BLOCK
    gate = jnp.einsum('bshd,bhnd->bhsn', q.astype(jnp.float32), k_mean)
    past = jnp.arange(nb)[None, :] < own_blk[:, None]
    gate = jnp.where(past[None, None], gate, NEG_INF)
    topk = min(MOBA_TOPK, nb)
    _, sel = lax.top_k(gate, topk)
    sel_valid = sel < own_blk[:, None]

    scale = HEAD_DIM ** -0.5
    n_qc = S // Q_CHUNK
    qs = q * scale
    q_c = qs.reshape(B, n_qc, Q_CHUNK, H, Dh).transpose(0, 1, 3, 2, 4).reshape(B * n_qc, H, Q_CHUNK, Dh)
    sel_c = sel.reshape(B, H, n_qc, Q_CHUNK, topk).transpose(0, 2, 1, 3, 4).reshape(B * n_qc, H, Q_CHUNK, topk)
    val_c = sel_valid.reshape(B, H, n_qc, Q_CHUNK, topk).transpose(0, 2, 1, 3, 4).reshape(B * n_qc, H, Q_CHUNK, topk)
    b_idx = jnp.repeat(jnp.arange(B, dtype=jnp.int32), n_qc)
    c_idx = jnp.tile(jnp.arange(n_qc, dtype=jnp.int32), B)
    h_ix = jnp.arange(H)[:, None, None]
    n_sel = topk * MOBA_BLOCK

    def query_block(args):
        b, c, qc, selc, validc = args
        kb = k_blk[b]
        vb = v_blk[b]
        k_sel = kb[h_ix, selc]
        v_sel = vb[h_ix, selc]
        s_sel = jnp.einsum('hqd,hqnld->hqnl', qc, k_sel).astype(jnp.float32)
        s_sel = jnp.where(validc[..., None], s_sel, NEG_INF).reshape(H, Q_CHUNK, n_sel)
        i = (c * Q_CHUNK) // MOBA_BLOCK
        k_own = kb[:, i]
        v_own = vb[:, i]
        q_pos = c * Q_CHUNK + jnp.arange(Q_CHUNK)
        k_pos = i * MOBA_BLOCK + jnp.arange(MOBA_BLOCK)
        s_own = jnp.einsum('hqd,hld->hql', qc, k_own).astype(jnp.float32)
        s_own = jnp.where(k_pos[None, None, :] <= q_pos[None, :, None], s_own, NEG_INF)
        probs = jax.nn.softmax(jnp.concatenate([s_sel, s_own], axis=-1), axis=-1).astype(v.dtype)
        p_sel = probs[..., :n_sel].reshape(H, Q_CHUNK, topk, MOBA_BLOCK)
        p_own = probs[..., n_sel:]
        return (jnp.einsum('hqnl,hqnld->hqd', p_sel, v_sel)
                + jnp.einsum('hql,hld->hqd', p_own, v_own))

    o = lax.map(query_block, (b_idx, c_idx, q_c, sel_c, val_c))
    return o.reshape(B, n_qc, H, Q_CHUNK, Dh).transpose(0, 1, 3, 2, 4).reshape(B, S, H * Dh)

def gmlp_spatial_gating(u, gv, ln_g, ln_b, w_s, b_s):
    B, S, _ = gv.shape
    vn = layer_norm(gv, ln_g, ln_b)
    nc = S // GMLP_CHUNK
    vc = vn.reshape(B, nc, GMLP_CHUNK, N_GMLP_GROUPS, GMLP_GROUP_DIM)
    causal = jnp.tril(jnp.ones((GMLP_CHUNK, GMLP_CHUNK), dtype=bool))
    w = jnp.where(causal[None], w_s, 0.0)
    mixed = jnp.einsum('gts,bcsgd->bctgd', w, vc) + b_s.T[None, None, :, :, None]
    return u * mixed.reshape(B, S, D_GMLP)

def setup_inputs(seed: int = 0) -> dict:
    key = jax.random.key(seed)
    ks = jax.random.split(key, 20)
    f32 = jnp.float32

    def nrm(k, shape, scale):
        return jax.random.normal(k, shape, f32) * scale

    def gain(k, shape):
        return 1.0 + 0.05 * jax.random.normal(k, shape, f32)

    return {
        "x": jax.random.normal(ks[0], (BATCH, SEQ, D_MODEL), f32),
        "p": jax.random.normal(ks[1], (DEPTH, BATCH, SEQ, D_PLE), f32),
        "mix_pre_g": gain(ks[2], (DEPTH, D_MODEL)),
        "w_in": nrm(ks[3], (DEPTH, D_MODEL, D_IN_PROJ), D_MODEL ** -0.5),
        "gmlp_ln_g": gain(ks[4], (DEPTH, D_GMLP)),
        "gmlp_ln_b": nrm(ks[5], (DEPTH, D_GMLP), 0.02),
        "w_s": nrm(ks[6], (DEPTH, N_GMLP_GROUPS, GMLP_CHUNK, GMLP_CHUNK), GMLP_CHUNK ** -0.5),
        "b_s": 1.0 + 0.1 * jax.random.normal(ks[7], (DEPTH, N_GMLP_GROUPS, GMLP_CHUNK), f32),
        "attn_out_g": gain(ks[8], (DEPTH, D_ATTN)),
        "gmlp_out_g": gain(ks[9], (DEPTH, D_GMLP)),
        "w_o": nrm(ks[10], (DEPTH, D_MIX, D_MODEL), D_MIX ** -0.5),
        "mix_post_g": gain(ks[11], (DEPTH, D_MODEL)),
        "mlp_pre_g": gain(ks[12], (DEPTH, D_MODEL)),
        "w_up": nrm(ks[13], (DEPTH, D_MODEL, D_FF), D_MODEL ** -0.5),
        "w_down": nrm(ks[14], (DEPTH, D_FF, D_MODEL), D_FF ** -0.5),
        "mlp_post_g": gain(ks[15], (DEPTH, D_MODEL)),
        "w_ple": nrm(ks[16], (DEPTH, D_PLE, D_MODEL), D_PLE ** -0.5),
        "w_ple_gate": nrm(ks[17], (DEPTH, D_MODEL, D_MODEL), D_MODEL ** -0.5),
        "b_ple_gate": nrm(ks[18], (DEPTH, D_MODEL), 0.02),
        "ple_post_g": gain(ks[19], (DEPTH, D_MODEL)),
    }

def reference(x, p, mix_pre_g, w_in, gmlp_ln_g, gmlp_ln_b, w_s, b_s, attn_out_g,
              gmlp_out_g, w_o, mix_post_g, mlp_pre_g, w_up, w_down, mlp_post_g,
              w_ple, w_ple_gate, b_ple_gate, ple_post_g):
    B, S, _ = x.shape
    pos = jnp.arange(S, dtype=jnp.int32)
    h = x
    for i in range(DEPTH):
        hn = rms_norm(h, mix_pre_g[i])
        proj = jnp.einsum('bsd,de->bse', hn, w_in[i])
        q, k, v, u, gv = jnp.split(
            proj, [D_ATTN, 2 * D_ATTN, 3 * D_ATTN, 3 * D_ATTN + D_GMLP], axis=-1)
        q = partial_rope(q.reshape(B, S, N_ATTN_HEADS, HEAD_DIM), pos)
        k = partial_rope(k.reshape(B, S, N_ATTN_HEADS, HEAD_DIM), pos)
        v = v.reshape(B, S, N_ATTN_HEADS, HEAD_DIM)
        attn_out = moba_attention(q, k, v)
        gmlp_out = gmlp_spatial_gating(jax.nn.gelu(u, approximate=False),
                                       jax.nn.gelu(gv, approximate=False),
                                       gmlp_ln_g[i], gmlp_ln_b[i], w_s[i], b_s[i])
        mixed = jnp.concatenate([rms_norm(attn_out, attn_out_g[i]),
                                 rms_norm(gmlp_out, gmlp_out_g[i])], axis=-1)
        h = h + rms_norm(jnp.einsum('bse,ed->bsd', mixed, w_o[i]), mix_post_g[i])
        hn = rms_norm(h, mlp_pre_g[i])
        ff = jnp.square(jax.nn.relu(jnp.einsum('bsd,df->bsf', hn, w_up[i])))
        h = h + rms_norm(jnp.einsum('bsf,fd->bsd', ff, w_down[i]), mlp_post_g[i])
        gate = jax.nn.sigmoid(jnp.einsum('bsd,de->bse', h, w_ple_gate[i]) + b_ple_gate[i])
        ple = jnp.einsum('bsp,pd->bsd', p[i], w_ple[i]) * gate
        h = h + rms_norm(ple, ple_post_g[i])
    return h


_drawn_inputs = setup_inputs


def setup_inputs(seed=0):
    import zlib

    import numpy as np

    out = dict(_drawn_inputs(seed))
    spreads = {}
    factors = {}
    for name, (base, spread) in spreads.items():
        noise = np.random.default_rng([zlib.crc32(name.encode()), seed]).standard_normal(out[name].shape)
        drawn = base * np.exp(spread * noise) if base else spread * noise
        out[name] = __import__('jax').numpy.asarray(drawn.astype(out[name].dtype))
    for name, factor in factors.items():
        out[name] = (out[name] * factor).astype(out[name].dtype)
    return out
```

```python
from contextlib import ExitStack

import concourse.bass as bass
from concourse import mybir

F32 = mybir.dt.float32
F32R = mybir.dt.float32r
BF16 = mybir.dt.bfloat16
ALU = mybir.AluOpType
ACT = mybir.ActivationFunctionType
AXIS_X = mybir.AxisListType.X

P = 128
D = 1024
SEQ = 512
TT = SEQ // P
KD = D // P
W = 512
HALVES = D // W
HEADS, DH = 8, 64
PAIRS = HEADS // 2
GROUPS, GD = 8, 64
D_PLE = 256
KP = D_PLE // P
D_FF = 4 * D
CHUNKS = D_FF // D
HALF_ROPE = DH // 4 // 2
EPS = 1e-6
NEG = -1e30
SCALE = DH ** -0.5

G_GV, G_U, G_Q, G_K, G_V, G_O0, G_O1, G_PLE, G_FF = range(9)
SLAB_PLE = 7 * KD
SLAB_FF = SLAB_PLE + HALVES * KP
SLABS_PER_CHUNK = 4 * KD
SLAB_GATE = SLAB_FF + CHUNKS * SLABS_PER_CHUNK
SLABS = SLAB_GATE + HALVES * KD
PAIRS_OF_SLABS = SLABS // 2
FIRST_PAIRS = KD // 2

BANK_S, BANK_PT, BANK_O = 3, 5, 7


def phase_one_results():
    names = []
    for n in range(20):
        names.append(("proj", n))
        if n in (8, 9):
            names += [("mix", 2 * (n - 8)), ("mix", 2 * (n - 8) + 1)]
        if 9 <= n <= 16:
            names.append(("qkT", n - 9))
        if 12 <= n <= 15:
            names.append(("gateT", n - 12))
    names += [("proj", n) for n in range(20, 26)]
    banks = {name: i % 3 for i, name in enumerate(names)}
    a, b, c = (banks["proj", n] for n in (20, 21, 22))
    late = [(("attnT", 0), 5), (("proj", 20), a), (("proj", 21), b), (("attnT", 1), 5),
            (("proj", 22), c), (("proj", 23), a), (("attnT", 2), 5), (("hT", 0), 5), (("hT", 1), 6),
            (("proj", 24), b), (("proj", 25), c), (("hT", 2), a), (("hT", 3), 6),
            (("attnT", 3), 5), (("proj", 26), 3), (("proj", 27), 4),
            (("ple", 0), 7), (("ple", 1), 6), (("ple", 2), 5), (("hT", 4), a), (("hT", 5), b),
            (("ple", 3), c), (("ple", 4), 7), (("ple", 5), 6), (("ple", 6), 5), (("ple", 7), a),
            (("hT", 6), 3), (("hT", 7), 4)]
    banks.update(late)
    return names[:-6] + [name for name, _ in late], banks


def tail_results():
    late = [(("down", 0), 5), (("down", 1), 6), (("down", 2), 7), (("h2T", 0), 1), (("h2T", 1), 2),
            (("down", 3), 0), (("h2T", 2), 3), (("h2T", 3), 4), (("gate", 0, 0), 5),
            (("h2T", 4), 6), (("h2T", 5), 7), (("gate", 1, 0), 0), (("h2T", 6), 1), (("h2T", 7), 2),
            (("gate", 0, 1), 3), (("gate", 1, 1), 4), (("gate", 2, 0), 5), (("gate", 2, 1), 6),
            (("gate", 3, 0), 7), (("gate", 3, 1), 0)]
    return [name for name, _ in late], dict(late)


GATE_ORDER = ((0, 0), (1, 0), (0, 1), (1, 1), (2, 0), (2, 1), (3, 0), (3, 1))
STEP_TILES = [(17, 0), (17, 4), (18, 0), (18, 4), (19, 0), (19, 4), (20, 0), (20, 4),
              (21, 0), (21, 4), (22, 0), (22, 4), (23, 0), (23, 4), (24, 0), (24, 4)]
STEP_SPLITS = {0: [G_O0 * KD + 2], 1: [G_O0 * KD + 4], 2: [G_O0 * KD + 6], 5: [G_O1 * KD],
               6: [G_O1 * KD + 2, G_O1 * KD + 4], 7: [G_O1 * KD + 6]}


def hymba_layer(nc, x, xT, pT, weights, columns, rope, ws, rows, out):
    phase1, bank1 = phase_one_results()
    tail, bank2 = tail_results()
    filled1 = {name: i + 1 for i, name in enumerate(phase1)}
    FILLED_FF = len(phase1)
    filled2 = {name: FILLED_FF + 16 * (CHUNKS - 1) + 12 + i + 1 for i, name in enumerate(tail)}

    with ExitStack() as ctx:
        top = [0]

        def place(name, shape, dt=F32, at=None):
            size = 2 if dt == BF16 else 4
            for n in shape[1:]:
                size *= n
            if at is None:
                at = top[0]
                top[0] += -(-size // 32) * 32
            return nc.alloc_sbuf_tensor_at(name, shape, dt, offset=at)

        base = nc.sbuf_base
        top[0] = -(-base // 32) * 32
        h = place("h", [P, TT, D])
        actT_hi = place("actT_hi", [P, KD, SEQ], F32R)
        actT_lo = place("actT_lo", [P, KD, SEQ], F32R)
        at_mixed_hi = top[0]
        mixT_hi = place("mixT_hi", [P, KD, SEQ], F32R)
        at_mixed_lo = top[0]
        mixT_lo = place("mixT_lo", [P, KD, SEQ], F32R)
        w_hi = place("w_hi", [P, 2 * KD, W], F32R)
        w_lo = place("w_lo", [P, 2 * KD, W], F32R)
        raw = place("raw", [P, 4, W])
        gain_post = place("gain_post", [P, D])
        work = place("work", [P, 2, W])
        junk = place("junk", [P, D])
        cols = place("cols", [P, columns.shape[1]])
        rope_sb = place("rope_sb", [P, TT, 2, 2 * HALF_ROPE])
        rope_tmp = place("rope_tmp", [P, 2, HEADS, 2 * HALF_ROPE])
        rinv = place("rinv", [P, HEADS])
        ident = place("ident", [P, P])
        ident_bf = place("ident_bf", [P, P], BF16)
        causal_bf = place("causal_bf", [P, P], BF16)
        stat = place("stat", [P, 114])
        rowsum = place("rowsum", [P, TT * PAIRS, 2])
        at_area = top[0]
        K = 1024
        qT = place("qT", [P, PAIRS, SEQ])
        kT = place("kT", [P, PAIRS, SEQ])
        v = place("v", [P, TT, W])
        probs = place("probs", [P, 2, 2, SEQ])
        probsT = place("probsT", [P, 2, TT, P])
        attn = place("attn", [P, W])
        assert top[0] <= nc.sbuf_usable_end
        xT_raw = place("xT_raw", [P, TT, KD, P], at=at_area)
        u = place("u", [P, TT, W], at=at_area + 24 * K)
        ln_gb = place("ln_gb", [P, 2, W], at=at_area + 32 * K)
        first_raw = [place("first_raw_a", [P, KD // 2, W], at=at_mixed_hi),
                     place("first_raw_b", [P, KD // 2, W], at=at_mixed_lo)]
        gv = place("gv", [P, TT, W], at=at_mixed_hi + 8 * K)
        wsT = place("wsT", [P, GROUPS, P], at=at_mixed_lo + 8 * K)
        ple = place("ple", [P, TT, D], at=at_area)
        acc = place("acc", [P, TT, D], at=at_area + 16 * K)
        pT_raw = place("pT_raw", [P, KP, SEQ], at=at_area + 16 * K)
        pT_hi = place("pT_hi", [P, KP, SEQ], F32R, at=at_area + 20 * K)
        pT_lo = place("pT_lo", [P, KP, SEQ], F32R, at=at_area + 24 * K)
        gate_rows = place("gate_rows", [P, 2, D], at=at_mixed_hi)

        psum = ctx.enter_context(nc.psum_tensor("psum", [P, 8, W], F32))

        mix_pre = lambda k: cols[:, k:k + 1]
        mlp_pre = lambda k: cols[:, 8 + k:9 + k]
        mixed_gain = lambda k: cols[:, 16 + k:17 + k]
        b_s = lambda g: cols[:, 24 + g:25 + g]
        minus_half = stat[:, 0:4]
        ss_x, rstd_x = stat[:, 4:8], stat[:, 8:12]
        ss_gm, rstd_gm = stat[:, 12:16], stat[:, 16:20]
        ss_at, rstd_at = stat[:, 20:24], stat[:, 24:28]
        ss_o, rstd_o = stat[:, 28:36], stat[:, 36:40]
        ss_h, rstd_h = stat[:, 40:44], stat[:, 44:48]
        ss_dn, rstd_dn = stat[:, 48:52], stat[:, 52:56]
        ss_pl, rstd_pl = stat[:, 56:64], stat[:, 64:68]
        pool_tmp = stat[:, 68:72]
        mean_var = stat[:, 72:80].rearrange("p (t c) -> p t c", c=2)
        rstd_ln = stat[:, 80:84]
        bn6 = lambda t: stat[:, 90 + 6 * t:96 + 6 * t]
        neg_max = stat[:, 84:86]
        row_max = stat[:, 86:88]

        def sem(name):
            return ctx.enter_context(nc.semaphore(name))

        xT_loaded = [sem(f"xT_loaded{t}") for t in range(TT)]
        x_loaded = [sem(f"x_loaded{t}") for t in range(TT)]
        first_loaded = [sem(f"first_loaded{k}") for k in range(KD)]
        raw_loaded = [sem(f"raw_loaded{j}") for j in range(2)]
        cols_loaded, rope_loaded, ws_loaded = sem("cols_loaded"), sem("rope_loaded"), sem("ws_loaded")
        ln_loaded, post_loaded, pT_loaded = sem("ln_loaded"), sem("post_loaded"), sem("pT_loaded")
        gate_rows_loaded, stored = sem("gate_rows_loaded"), sem("stored")
        slab_hi, slab_lo, slab_used = sem("slab_hi"), sem("slab_lo"), sem("slab_used")
        filled, act_drained, dve_drained = sem("filled"), sem("act_drained"), sem("dve_drained")
        constants_set, ws_masked, acc_zeroed = sem("constants_set"), sem("ws_masked"), sem("acc_zeroed")
        xT_hi_done, xT_lo_done, x_squared, x_rstd = (sem("xT_hi_done"), sem("xT_lo_done"),
                                                     sem("x_squared"), sem("x_rstd"))
        ln_stats, ln_mean, ln_rstd, ln_centred, vn_ready = (sem("ln_stats"), sem("ln_mean"),
                                                            sem("ln_rstd"), sem("ln_centred"),
                                                            sem("vn_ready"))
        roped = sem("roped")
        gm_squared, gm_rstd, gm_scaled = sem("gm_squared"), sem("gm_rstd"), sem("gm_scaled")
        turned_hi = sem("turned_hi")
        scores_ready, max_found, max_ready, probs_ready = (sem("scores_ready"), sem("max_found"),
                                                           sem("max_ready"), sem("probs_ready"))
        pt_filled, pt0_drained, pt1_drained, pv_done = (sem("pt_filled"), sem("pt0_drained"),
                                                        sem("pt1_drained"), sem("pv_done"))
        rinv_ready, attn_ready, at_squared, at_rstd, at_scaled = (
            sem("rinv_ready"), sem("attn_ready"), sem("at_squared"), sem("at_rstd"), sem("at_scaled"))
        o_squared, o_rstd, o_normed = sem("o_squared"), sem("o_rstd"), sem("o_normed")
        h1_squared, h1_rstd, hn_ready = sem("h1_squared"), sem("h1_rstd"), sem("hn_ready")
        pT_hi_done, pT_lo_done = sem("pT_hi_done"), sem("pT_lo_done")
        relu_done, ff_squared, ff_hi_done = sem("relu_done"), sem("ff_squared"), sem("ff_hi_done")
        dn_squared, dn_rstd, dn_normed, h2_ready = (sem("dn_squared"), sem("dn_rstd"),
                                                    sem("dn_normed"), sem("h2_ready"))
        sig_done, pl_gated, pl_squared, pl_rstd, pl_normed, out_ready = (
            sem("sig_done"), sem("pl_gated"), sem("pl_squared"), sem("pl_rstd"),
            sem("pl_normed"), sem("out_ready"))
        pool_chain = sem("pool_chain")

        def ring(slab):
            if slab < SLAB_PLE:
                return (slab // KD % 2) * KD + slab % KD
            if slab < SLAB_FF:
                return KD + slab - SLAB_PLE
            return ((slab - SLAB_FF) // KD % 2) * KD + (slab - SLAB_FF) % KD

        def gain_of(slab):
            if slab < G_O0 * KD:
                return mix_pre(slab % KD)
            if slab < SLAB_PLE:
                return mixed_gain(slab % KD)
            i = (slab - SLAB_FF) % SLABS_PER_CHUNK
            if SLAB_FF <= slab < SLAB_GATE and i < 2 * KD:
                return mlp_pre(i % KD)
            return None

        def raw_place(slab):
            if slab < KD:
                return first_raw[slab // 4][:, slab % 4, :]
            return raw[:, slab % 4, :]

        drained = {}

        block = ctx.enter_context(nc.Block())

        @block.vector
        def _(dve):
            count = [0]

            def drained_by_dve(instruction, name):
                instruction.then_inc(dve_drained, 1)
                count[0] += 1
                drained[name] = (dve_drained, count[0])

            def split_lo(gain, source, place_at):
                high = w_hi[:, place_at, :].bitcast(F32)
                if gain is None:
                    nc.vector.tensor_tensor(w_lo[:, place_at, :], source, high, ALU.subtract
                                            ).then_inc(slab_lo, 1)
                else:
                    nc.vector.scalar_tensor_tensor(out=w_lo[:, place_at, :], in0=source, scalar=gain,
                                                   in1=high, op0=ALU.mult, op1=ALU.subtract
                                                   ).then_inc(slab_lo, 1)

            def splits(slab):
                for s in (slab, slab + 1):
                    dve.wait_ge(slab_hi, s + 1)
                    split_lo(gain_of(s), raw_place(s), ring(s))

            turned = [0]

            def turn_lo(name, target, high, bank):
                turned[0] += 1
                dve.wait_ge(turned_hi, turned[0])
                drained_by_dve(nc.vector.tensor_tensor(
                    target, psum[:, bank, :].rearrange("p (k n) -> p k n", n=P),
                    high.bitcast(F32), ALU.subtract), name)

            def xT_lo(t):
                dve.wait_ge(xT_hi_done, t + 1)
                cut = slice(t * P, (t + 1) * P)
                nc.vector.tensor_tensor(actT_lo[:, :, cut], xT_raw[:, t], actT_hi[:, :, cut].bitcast(F32),
                                        ALU.subtract).then_inc(xT_lo_done, 1)

            xT_lo(0)
            for k in range(KD):
                dve.wait_ge(slab_hi, k + 1)
                split_lo(gain_of(k), raw_place(k), k)
                if k == 3:
                    xT_lo(1)
            xT_lo(2)
            xT_lo(3)
            splits(KD)

            def ln_stats_of(t):
                dve.wait_ge(act_drained, t + 1)
                nc.vector.bn_stats(bn6(t), gv[:, t, :]).then_inc(ln_stats, 1)
                dve.wait_ge(ln_stats, t + 1)
                nc.vector.bn_aggr(mean_var[:, t, :], bn6(t)).then_inc(ln_mean, 1)

            def ln_centre(t):
                dve.wait_ge(ln_rstd, t + 1)
                nc.vector.tensor_scalar(gv[:, t, :], gv[:, t, :], mean_var[:, t, 0:1],
                                        rstd_ln[:, t:t + 1], ALU.subtract, ALU.mult
                                        ).then_inc(ln_centred, 1)

            def mix_drain(i):
                bank = psum[:, bank1["mix", i], :]
                dve.wait_ge(filled, filled1["mix", i])
                if i == 0:
                    dve.wait_ge(act_drained, 2 * TT)
                for a in range(2):
                    g = 2 * i + a
                    part = u[:, :, g * GD:(g + 1) * GD]
                    last = nc.vector.scalar_tensor_tensor(
                        out=part, in0=bank[:, a * 256:(a + 1) * 256].rearrange("p (t d) -> p t d", d=GD),
                        scalar=b_s(g), in1=part, op0=ALU.add, op1=ALU.mult)
                drained_by_dve(last, ("mix", i))

            def qkT_drain(i):
                target = (qT, kT)[i // TT][:, :, i % TT * P:(i % TT + 1) * P]
                dve.wait_ge(filled, filled1["qkT", i])
                if i == 0:
                    dve.wait_ge(xT_lo_done, TT)
                drained_by_dve(nc.vector.tensor_copy(
                    target, psum[:, bank1["qkT", i], :].rearrange("p (k n) -> p k n", n=P)), ("qkT", i))

            def gate_turn_lo(t):
                cut = slice(t * P, (t + 1) * P)
                turn_lo(("gateT", t), mixT_lo[:, 0:4, cut], mixT_hi[:, 0:4, cut], bank1["gateT", t])

            for n in range(16):
                group, j = divmod(n, TT)
                if n:
                    splits((group + 1) * KD + 2 * j)
                if n < TT:
                    ln_stats_of(n)
                if 1 <= n <= TT:
                    ln_centre(n - 1)
                if n in (9, 10):
                    mix_drain(2 * (n - 9))
                    mix_drain(2 * (n - 9) + 1)
                if n >= 10:
                    qkT_drain(n - 10)
                if n == 11:
                    dve.wait_ge(gm_rstd, 1)
                    for t in range(TT):
                        nc.vector.tensor_scalar(u[:, t, :], u[:, t, :], rstd_gm[:, t:t + 1], None,
                                                ALU.mult).then_inc(gm_scaled, 1)
                if 12 <= n <= 15:
                    gate_turn_lo(n - 12)
            splits(G_O0 * KD)
            qkT_drain(6)
            qkT_drain(7)

            def row_maxima(unit):
                n = (unit // PAIRS + 1) * P
                dve.wait_ge(scores_ready, unit + 1)
                if unit >= 1:
                    dve.wait_ge(probs_ready, unit)
                nc.vector.tensor_reduce(row_max, psum[:, BANK_S:BANK_S + 2, 0:n], AXIS_X, ALU.max
                                        ).then_inc(max_found, 1)
                dve.wait_ge(max_found, unit + 1)
                nc.vector.tensor_scalar(neg_max, row_max, -SCALE, None, ALU.mult).then_inc(max_ready, 1)

            def drain_pt0(unit):
                n = (unit // PAIRS + 1) * P
                dve.wait_ge(pt_filled, 2 * unit + 1)
                nc.vector.tensor_copy(probsT[:, 0].rearrange("p k q -> p (k q)")[:, 0:n],
                                      psum[:, BANK_PT, 0:n]).then_inc(pt0_drained, 1)

            def attn_rows(qt):
                dve.wait_ge(pv_done, PAIRS * (qt + 1))
                sums = rowsum[:, PAIRS * qt:PAIRS * (qt + 1), :].rearrange("p a b -> p (a b)")
                nc.vector.reciprocal(rinv[:], sums).then_inc(rinv_ready, 1)
                dve.wait_ge(rinv_ready, qt + 1)
                nc.vector.tensor_tensor(attn[:].rearrange("p (h d) -> p h d", d=DH),
                                        psum[:, BANK_O, :].rearrange("p (h d) -> p h d", d=DH),
                                        rinv[:, :, None].to_broadcast([P, HEADS, DH]), ALU.mult
                                        ).then_inc(attn_ready, 1)

            def attn_scale(qt):
                dve.wait_ge(at_rstd, qt + 1)
                nc.vector.tensor_scalar(attn[:], attn[:], rstd_at[:, qt:qt + 1], None, ALU.mult
                                        ).then_inc(at_scaled, 1)

            def attn_turn_lo(qt):
                cut = slice(qt * P, (qt + 1) * P)
                turn_lo(("attnT", qt), mixT_lo[:, 4:8, cut], mixT_hi[:, 4:8, cut], bank1["attnT", qt])

            def add_mixed(t):
                if t == 0:
                    dve.wait_ge(post_loaded, 16)
                dve.wait_ge(o_rstd, t + 1)
                for half in range(HALVES):
                    n = 20 + 2 * t + half
                    bank = psum[:, bank1["proj", n], :]
                    cut = slice(half * W, (half + 1) * W)
                    nc.vector.scalar_tensor_tensor(out=bank, in0=bank, scalar=rstd_o[:, t:t + 1],
                                                   in1=gain_post[:, cut], op0=ALU.mult, op1=ALU.mult
                                                   ).then_inc(o_normed, 1)
                for half in range(HALVES):
                    n = 20 + 2 * t + half
                    bank = psum[:, bank1["proj", n], :]
                    cut = slice(half * W, (half + 1) * W)
                    dve.wait_ge(o_normed, 2 * t + half + 1)
                    drained_by_dve(nc.vector.tensor_tensor(h[:, t, cut], h[:, t, cut], bank, ALU.add),
                                   ("proj", n))

            def hn_turn_lo(i):
                t, j = divmod(i, 2)
                cut = slice(t * P, (t + 1) * P)
                turn_lo(("hT", i), actT_lo[:, 4 * j:4 * j + 4, cut], actT_hi[:, 4 * j:4 * j + 4, cut],
                        bank1["hT", i])

            for step in range(TT * PAIRS):
                if step >= 6 and step % 4 == 2:
                    attn_turn_lo(step // 4 - 1)
                if step == 15:
                    hn_turn_lo(0)
                    hn_turn_lo(1)
                row_maxima(step)
                if step >= 1:
                    drain_pt0(step - 1)
                if step >= 5 and step % 4 == 1:
                    attn_scale(step // 4 - 1)
                for slab in STEP_SPLITS.get(step, ()):
                    splits(slab)
                if step >= 4 and step % 4 == 0:
                    attn_rows(step // 4 - 1)
                if step == 11:
                    add_mixed(0)
                if step == 15:
                    add_mixed(1)
            drain_pt0(15)
            attn_rows(3)
            attn_scale(3)
            hn_turn_lo(2)
            hn_turn_lo(3)
            attn_turn_lo(3)
            add_mixed(2)
            dve.wait_ge(pT_hi_done, 1)
            nc.vector.tensor_tensor(pT_lo[:], pT_raw[:], pT_hi[:].bitcast(F32), ALU.subtract
                                    ).then_inc(pT_lo_done, 1)
            for i in range(2):
                splits(SLAB_PLE + 2 * i)

            def ple_drain(i):
                half, t = divmod(i, TT)
                dve.wait_ge(filled, filled1["ple", i])
                drained_by_dve(nc.vector.tensor_copy(ple[:, t, half * W:(half + 1) * W],
                                                     psum[:, bank1["ple", i], :]), ("ple", i))

            add_mixed(3)
            for i in range(2):
                splits(SLAB_FF + 2 * i)
            for i in range(3):
                ple_drain(i)
            hn_turn_lo(4)
            hn_turn_lo(5)
            for i in range(2, 4):
                splits(SLAB_FF + 2 * i)
            for i in range(3, 8):
                ple_drain(i)
            hn_turn_lo(6)
            hn_turn_lo(7)
            before_mlp = count[0]
            drained["before_mlp"] = (dve_drained, before_mlp)

            def mlp_tiles(c, tiles, gate_next=False):
                for m in tiles:
                    i, j = divmod(m, TT)
                    off = KD * (i + 1) + 2 * j
                    s = SLAB_FF + off
                    place_at = ((i + 1) % 2) * KD + 2 * j
                    gain = [mlp_pre(2 * j + a) if i in (0, 3) else None for a in range(2)]
                    if gate_next:
                        gain = [None, None]
                    bank = psum[:, (m + 1) % 8, :]

                    def lo(a):
                        dve.wait_ge(slab_hi, s + a + 1 + SLABS_PER_CHUNK * c)
                        split_lo(gain[a], raw[:, (s + a) % 4, :], place_at + a)

                    lo(0)
                    if m < 8:
                        dve.wait_ge(relu_done, m + 1 + 8 * c)
                        nc.vector.scalar_tensor_tensor(out=bank, in0=bank, scalar=0.0,
                                                       in1=work[:, m % 2, :], op0=ALU.max, op1=ALU.mult
                                                       ).then_inc(ff_squared, 1)
                        lo(1)
                        dve.wait_ge(ff_hi_done, m + 1 + 8 * c)
                        nc.vector.tensor_tensor(mixT_lo[:, m, :], bank, mixT_hi[:, m, :].bitcast(F32),
                                                ALU.subtract).then_inc(dve_drained, 1)
                        continue
                    lo(1)
                    half, t = divmod(m - 8, TT)
                    part = acc[:, t, half * W:(half + 1) * W]
                    if m == 8:
                        dve.wait_ge(acc_zeroed, 1)
                    if gate_next:
                        dve.wait_ge(filled, filled2["down", t])
                    else:
                        dve.wait_ge(filled, FILLED_FF + m + 1 + 16 * c)
                    nc.vector.tensor_tensor(part, part, bank, ALU.add).then_inc(dve_drained, 1)

            with dve.Fori(0, CHUNKS - 1) as c:
                mlp_tiles(c, range(16))
            last = CHUNKS - 1
            mlp_tiles(last, range(12))
            count[0] += 16 * CHUNKS - TT

            def add_mlp(t):
                if t == 0:
                    dve.wait_ge(post_loaded, 32)
                dve.wait_ge(dn_rstd, t + 1)
                nc.vector.scalar_tensor_tensor(out=acc[:, t, :], in0=acc[:, t, :],
                                               scalar=rstd_dn[:, t:t + 1], in1=gain_post[:],
                                               op0=ALU.mult, op1=ALU.mult).then_inc(dn_normed, 1)
                dve.wait_ge(dn_normed, t + 1)
                nc.vector.tensor_tensor(h[:, t, :], h[:, t, :], acc[:, t, :], ALU.add
                                        ).then_inc(h2_ready, 1)

            def h2_turn_lo(i):
                t, j = divmod(i, 2)
                cut = slice(t * P, (t + 1) * P)
                turn_lo(("h2T", i), actT_lo[:, 4 * j:4 * j + 4, cut], actT_hi[:, 4 * j:4 * j + 4, cut],
                        bank2["h2T", i])

            def gate_bias(i, t, half):
                cut = slice(half * W, (half + 1) * W)
                if i == 0:
                    dve.wait_ge(gate_rows_loaded, 16)
                dve.wait_ge(filled, filled2["gate", t, half])
                drained_by_dve(nc.vector.tensor_tensor(acc[:, t, cut], psum[:, bank2["gate", t, half], :],
                                                       gate_rows[:, 0, cut], ALU.add), ("gate", t, half))

            def gate_ple(i, t, half):
                cut = slice(half * W, (half + 1) * W)
                dve.wait_ge(sig_done, i + 1)
                nc.vector.tensor_tensor(acc[:, t, cut], acc[:, t, cut], ple[:, t, cut], ALU.mult
                                        ).then_inc(pl_gated, 1)

            def add_ple(n, t):
                dve.wait_ge(pl_rstd, n + 1)
                nc.vector.scalar_tensor_tensor(out=acc[:, t, :], in0=acc[:, t, :],
                                               scalar=rstd_pl[:, t:t + 1], in1=gate_rows[:, 1, :],
                                               op0=ALU.mult, op1=ALU.mult).then_inc(pl_normed, 1)
                dve.wait_ge(pl_normed, n + 1)
                nc.vector.tensor_tensor(h[:, t, :], h[:, t, :], acc[:, t, :], ALU.add
                                        ).then_inc(out_ready, 1)

            def tail_down(t):
                mlp_tiles(last, (12 + t,), gate_next=True)
                count[0] += 1
                drained["down", t] = (dve_drained, count[0])

            tail_down(0)
            tail_down(1)
            add_mlp(0)
            tail_down(2)
            add_mlp(1)
            h2_turn_lo(0)
            h2_turn_lo(1)
            tail_down(3)
            add_mlp(2)
            h2_turn_lo(2)
            h2_turn_lo(3)
            splits(SLAB_GATE + KD)
            add_mlp(3)
            h2_turn_lo(4)
            h2_turn_lo(5)
            splits(SLAB_GATE + KD + 2)
            splits(SLAB_GATE + KD + 4)
            h2_turn_lo(6)
            h2_turn_lo(7)
            splits(SLAB_GATE + KD + 6)
            finished = 0
            for i, (t, half) in enumerate(GATE_ORDER):
                gate_bias(i, t, half)
                gate_ple(i, t, half)
                if half == 1:
                    add_ple(finished, t)
                    finished += 1

        @block.scalar
        def _(act):
            act.dma_start(cols[:], columns).then_inc(cols_loaded, 16)
            act.dma_start(ln_gb[:], rows["ln"]).then_inc(ln_loaded, 16)
            act.dma_start(wsT[:], ws).then_inc(ws_loaded, 16)
            act.dma_start(rope_sb[:], rope).then_inc(rope_loaded, 16)
            act.dma_start(gain_post[:], rows["mix_post"]).then_inc(post_loaded, 16)

            def split_hi(slab, gain, source, place_at):
                if gain is None:
                    nc.scalar.activation(w_hi[:, place_at, :], source, ACT.Copy).then_inc(slab_hi, 1)
                else:
                    nc.scalar.activation(w_hi[:, place_at, :], source, ACT.Copy,
                                         scale=gain).then_inc(slab_hi, 1)

            def split_hi_pair(slab, free_at):
                pair = slab // 2
                act.wait_ge(raw_loaded[pair % 2], 16 * ((pair - FIRST_PAIRS) // 2 + 1))
                if free_at:
                    act.wait_ge(slab_used, free_at)
                for s in (slab, slab + 1):
                    split_hi(s, gain_of(s), raw_place(s), ring(s))

            def splits(slab):
                split_hi_pair(slab, slab - 14 if slab >= 2 * KD else 0)

            def turn_hi(name, target, bank):
                act.wait_ge(filled, name)
                nc.scalar.activation(target, psum[:, bank, :].rearrange("p (k n) -> p k n", n=P),
                                     ACT.Copy).then_inc(turned_hi, 1)

            junk_written = []
            squares = {}

            def square(source, sums, done):
                if junk_written:
                    act.wait_ge(*junk_written[-1])
                nc.scalar.activation(junk[:, 0:source.shape[-1]], source, ACT.Square,
                                     accum_out=sums).then_inc(done, 1)
                squares[done.name] = squares.get(done.name, 0) + 1
                junk_written.append((done, squares[done.name]))

            def square_x(t):
                act.wait_ge(x_loaded[t], 16)
                square(h[:, t, :], ss_x[:, t:t + 1], x_squared)

            def xT_hi(t):
                act.wait_ge(xT_loaded[t], 16)
                nc.scalar.activation(actT_hi[:, :, t * P:(t + 1) * P], xT_raw[:, t], ACT.Copy
                                     ).then_inc(xT_hi_done, 1)

            xT_hi(0)
            act.wait_ge(cols_loaded, 16)
            for k in range(KD):
                act.wait_ge(first_loaded[k], 16)
                split_hi(k, gain_of(k), raw_place(k), k)
                if k == 3:
                    xT_hi(1)
            square_x(0)
            xT_hi(2)
            square_x(1)
            xT_hi(3)
            splits(KD)

            def proj_drain(n):
                group, t = divmod(n, TT)
                bank = psum[:, bank1["proj", n], :]
                if n < TT:
                    act.wait_ge(x_rstd, t + 1)
                act.wait_ge(filled, filled1["proj", n])
                rstd = rstd_x[:, t:t + 1]
                if group == G_GV:
                    if t == 0:
                        act.wait_ge(ws_loaded, 16)
                    last = nc.scalar.activation(gv[:, t, :], bank, ACT.Gelu, scale=rstd)
                elif group == G_U:
                    if t == 0:
                        act.wait_ge(xT_lo_done, TT)
                    last = nc.scalar.activation(u[:, t, :], bank, ACT.Gelu, scale=rstd)
                elif group in (G_Q, G_K):
                    i = n - 2 * TT
                    if i >= 2:
                        act.wait_ge(filled, filled1["qkT", i - 2])
                    last = nc.scalar.activation(work[:, i % 2, :], bank, ACT.Copy, scale=rstd)
                else:
                    last = nc.scalar.activation(v[:, t, :], bank, ACT.Copy, scale=rstd)
                last.then_inc(act_drained, 1)
                drained["proj", n] = (act_drained, n + 1)

            for n in range(16):
                group, j = divmod(n, TT)
                if n:
                    splits((group + 1) * KD + 2 * j)
                if n in (0, 1):
                    square_x(n + 2)
                if n == 10:
                    act.wait_ge(*drained["mix", 3])
                    for t in range(TT):
                        square(u[:, t, :], ss_gm[:, t:t + 1], gm_squared)
                proj_drain(n)
                if 12 <= n <= 15:
                    t = n - 12
                    turn_hi(filled1["gateT", t], mixT_hi[:, 0:4, t * P:(t + 1) * P],
                            bank1["gateT", t])
            splits(G_O0 * KD)
            proj_drain(16)

            def softmax(unit):
                n = (unit // PAIRS + 1) * P
                act.wait_ge(max_ready, unit + 1)
                for s in range(2):
                    last = nc.scalar.activation(probs[:, unit % 2, s, 0:n], psum[:, BANK_S + s, 0:n],
                                                ACT.Exp, bias=neg_max[:, s:s + 1], scale=SCALE,
                                                accum_out=rowsum[:, unit, s:s + 1])
                last.then_inc(probs_ready, 1)

            def drain_pt1(unit):
                n = (unit // PAIRS + 1) * P
                act.wait_ge(pt_filled, 2 * unit + 2)
                nc.scalar.activation(probsT[:, 1].rearrange("p k q -> p (k q)")[:, 0:n],
                                     psum[:, BANK_PT + 1, 0:n], ACT.Copy).then_inc(pt1_drained, 1)

            def square_attn(qt):
                act.wait_ge(attn_ready, qt + 1)
                square(attn[:], ss_at[:, qt:qt + 1], at_squared)

            def attn_turn_hi(qt):
                turn_hi(filled1["attnT", qt], mixT_hi[:, 4:8, qt * P:(qt + 1) * P], bank1["attnT", qt])

            def square_out(t):
                for half in range(HALVES):
                    n = 20 + 2 * t + half
                    act.wait_ge(filled, filled1["proj", n])
                    square(psum[:, bank1["proj", n], :], ss_o[:, 2 * t + half:2 * t + half + 1], o_squared)

            def norm_h1(t):
                act.wait_ge(*drained["proj", 21 + 2 * t])
                square(h[:, t, :], ss_h[:, t:t + 1], h1_squared)
                act.wait_ge(h1_rstd, t + 1)
                if t == 0:
                    act.wait_ge(filled, filled1["qkT", 7])
                else:
                    act.wait_ge(filled, filled1["hT", 2 * t - 1])
                nc.scalar.activation(work[:].rearrange("p a n -> p (a n)"), h[:, t, :], ACT.Copy,
                                     scale=rstd_h[:, t:t + 1]).then_inc(hn_ready, 1)

            def hn_turn_hi(i):
                t, j = divmod(i, 2)
                turn_hi(filled1["hT", i], actT_hi[:, 4 * j:4 * j + 4, t * P:(t + 1) * P], bank1["hT", i])

            for step in range(TT * PAIRS):
                if step >= 6 and step % 4 == 2:
                    attn_turn_hi(step // 4 - 1)
                if step == 15:
                    hn_turn_hi(0)
                    hn_turn_hi(1)
                if step >= 1:
                    drain_pt1(step - 1)
                softmax(step)
                for slab in STEP_SPLITS.get(step, ()):
                    splits(slab)
                if step in (1, 3, 5):
                    proj_drain(17 + step // 2)
                if step == 10:
                    square_out(0)
                if step == 12:
                    norm_h1(0)
                if step >= 4 and step % 4 == 0:
                    square_attn(step // 4 - 1)
                if step == 14:
                    square_out(1)
            drain_pt1(15)
            norm_h1(1)
            square_attn(3)
            act.wait_ge(pv_done, 16)
            act.dma_start(pT_raw[:], pT).then_inc(pT_loaded, 16)
            hn_turn_hi(2)
            hn_turn_hi(3)
            square_out(2)
            attn_turn_hi(3)
            act.wait_ge(pT_loaded, 16)
            nc.scalar.activation(pT_hi[:], pT_raw[:], ACT.Copy).then_inc(pT_hi_done, 1)
            norm_h1(2)
            for i in range(2):
                splits(SLAB_PLE + 2 * i)
            square_out(3)
            for i in range(2):
                split_hi_pair(SLAB_FF + 2 * i, G_O1 * KD + 2 * i + 2)
            hn_turn_hi(4)
            hn_turn_hi(5)
            norm_h1(3)
            for i in range(2, 4):
                split_hi_pair(SLAB_FF + 2 * i, G_O1 * KD + 2 * i + 2)
            act.wait_ge(*drained["proj", 27])
            act.dma_start(gain_post[:], rows["mlp_post"]).then_inc(post_loaded, 16)
            hn_turn_hi(6)
            hn_turn_hi(7)
            act.wait_ge(slab_used, SLAB_FF)

            def mlp_tiles(c, tiles, gate_next=False):
                for m in tiles:
                    i, j = divmod(m, TT)
                    off = KD * (i + 1) + 2 * j
                    s = SLAB_FF + off
                    act.wait_ge(raw_loaded[s // 2 % 2],
                                16 * ((s // 2 - FIRST_PAIRS) // 2 + 1) + 16 * KD * c)
                    act.wait_ge(slab_used, s - 14 + SLABS_PER_CHUNK * c)
                    place_at = ((i + 1) % 2) * KD + 2 * j
                    gain = [mlp_pre(2 * j + a) if i in (0, 3) else None for a in range(2)]
                    if gate_next:
                        gain = [None, None]
                    split_hi(None, gain[0], raw[:, s % 4, :], place_at)
                    if m >= 8:
                        split_hi(None, gain[1], raw[:, (s + 1) % 4, :], place_at + 1)
                        continue
                    bank = psum[:, (m + 1) % 8, :]
                    relu = work[:, m % 2, :]
                    act.wait_ge(filled, FILLED_FF + m + 1 + 16 * c)
                    if m >= 2:
                        act.wait_ge(ff_squared, m - 1 + 8 * c)
                    nc.scalar.activation(relu, bank, ACT.Relu).then_inc(relu_done, 1)
                    split_hi(None, gain[1], raw[:, (s + 1) % 4, :], place_at + 1)
                    act.wait_ge(ff_squared, m + 1 + 8 * c)
                    nc.scalar.activation(mixT_hi[:, m, :], bank, ACT.Copy).then_inc(ff_hi_done, 1)

            with act.Fori(0, CHUNKS - 1) as c:
                mlp_tiles(c, range(16))
            last = CHUNKS - 1
            mlp_tiles(last, range(12))

            def square_down(t):
                act.wait_ge(*drained["down", t])
                square(acc[:, t, :], ss_dn[:, t:t + 1], dn_squared)

            def h2_turn_hi(i):
                t, j = divmod(i, 2)
                turn_hi(filled2["h2T", i], actT_hi[:, 4 * j:4 * j + 4, t * P:(t + 1) * P], bank2["h2T", i])

            def sigmoid(i, t, half):
                act.wait_ge(*drained["gate", t, half])
                z = acc[:, t, half * W:(half + 1) * W]
                nc.scalar.activation(z, z, ACT.Sigmoid).then_inc(sig_done, 1)

            def square_ple(i, t, half):
                act.wait_ge(pl_gated, i + 1)
                square(acc[:, t, half * W:(half + 1) * W], ss_pl[:, 2 * t + half:2 * t + half + 1], pl_squared)

            mlp_tiles(last, (12, 13), gate_next=True)
            square_down(0)
            mlp_tiles(last, (14,), gate_next=True)
            square_down(1)
            mlp_tiles(last, (15,), gate_next=True)
            h2_turn_hi(0)
            h2_turn_hi(1)
            square_down(2)
            act.wait_ge(filled, filled2["down", 3])
            act.dma_start(gate_rows[:], rows["gate"]).then_inc(gate_rows_loaded, 16)
            h2_turn_hi(2)
            h2_turn_hi(3)
            square_down(3)
            splits(SLAB_GATE + KD)
            h2_turn_hi(4)
            h2_turn_hi(5)
            splits(SLAB_GATE + KD + 2)
            splits(SLAB_GATE + KD + 4)
            h2_turn_hi(6)
            h2_turn_hi(7)
            splits(SLAB_GATE + KD + 6)
            for i, (t, half) in enumerate(GATE_ORDER):
                sigmoid(i, t, half)
                square_ple(i, t, half)

        @block.gpsimd
        def _(pool):
            done = [0]

            def after(instruction):
                done[0] += 1
                instruction.then_inc(pool_chain, 1)
                pool.wait_ge(pool_chain, done[0])

            nc.gpsimd.memset(minus_half, -0.5).then_inc(constants_set, 1)
            after(nc.gpsimd.memset(ident[:], 0.0))
            nc.gpsimd.affine_select(out=ident[:], in_=ident[:], compare_op=ALU.not_equal, fill=1.0, base=0,
                                    pattern=[[-1, P]], channel_multiplier=1).then_inc(constants_set, 1)
            after(nc.gpsimd.memset(ident_bf[:], 0.0))
            nc.gpsimd.affine_select(out=ident_bf[:], in_=ident_bf[:], compare_op=ALU.not_equal, fill=1.0,
                                    base=0, pattern=[[-1, P]], channel_multiplier=1
                                    ).then_inc(constants_set, 1)
            after(nc.gpsimd.memset(causal_bf[:], 0.0))
            nc.gpsimd.affine_select(out=causal_bf[:], in_=causal_bf[:], compare_op=ALU.is_ge, fill=NEG,
                                    base=0, pattern=[[-1, P]], channel_multiplier=1
                                    ).then_inc(constants_set, 1)
            pool.wait_ge(constants_set, 4)

            def rstd(target, sums, n, ready, halves=None):
                width = target.shape[1]
                tmp = pool_tmp[:, 0:width]
                if halves is not None:
                    after(nc.gpsimd.tensor_tensor(tmp, sums, halves, ALU.add))
                    sums = tmp
                after(nc.gpsimd.tensor_scalar(tmp, sums, 1.0 / n, EPS, ALU.mult, ALU.add))
                nc.gpsimd.tensor_tensor(target, tmp, minus_half[:, 0:width], ALU.pow).then_inc(ready, 1)
                pool.wait_ge(ready, passed(ready))

            seen = {}

            def passed(ready):
                seen[id(ready)] = seen.get(id(ready), 0) + 1
                return seen[id(ready)]

            for t in range(TT):
                pool.wait_ge(x_squared, t + 1)
                rstd(rstd_x[:, t:t + 1], ss_x[:, t:t + 1], D, x_rstd)
                if t == 0:
                    pool.wait_ge(ws_loaded, 16)
                    nc.gpsimd.affine_select(out=wsT[:], in_=wsT[:], compare_op=ALU.is_ge, fill=0.0, base=0,
                                            pattern=[[0, GROUPS], [1, P]], channel_multiplier=-1
                                            ).then_inc(ws_masked, 1)

            pool.wait_ge(ln_loaded, 16)
            for t in range(TT):
                pool.wait_ge(ln_mean, t + 1)
                rstd(rstd_ln[:, t:t + 1], mean_var[:, t, 1:2], 1, ln_rstd)
                pool.wait_ge(ln_centred, t + 1)
                after(nc.gpsimd.tensor_tensor(gv[:, t, :], gv[:, t, :], ln_gb[:, 0, :], ALU.mult))
                nc.gpsimd.tensor_tensor(gv[:, t, :], gv[:, t, :], ln_gb[:, 1, :], ALU.add
                                        ).then_inc(vn_ready, 1)

            def rotate(i):
                t = i % TT
                rows_ = work[:, i % 2, :].rearrange("p (h d) -> p h d", d=DH)
                both, first, second = (rows_[:, :, 0:2 * HALF_ROPE], rows_[:, :, 0:HALF_ROPE],
                                       rows_[:, :, HALF_ROPE:2 * HALF_ROPE])
                cos = rope_sb[:, t:t + 1, 0, :].to_broadcast([P, HEADS, 2 * HALF_ROPE])
                sin = rope_sb[:, t:t + 1, 1, 0:HALF_ROPE].to_broadcast([P, HEADS, HALF_ROPE])
                pool.wait_ge(act_drained, 2 * TT + i + 1)
                nc.gpsimd.tensor_tensor(rope_tmp[:, 0], both, cos, ALU.mult)
                nc.gpsimd.tensor_tensor(rope_tmp[:, 1, :, HALF_ROPE:], first, sin, ALU.mult)
                after(nc.gpsimd.tensor_tensor(rope_tmp[:, 1, :, 0:HALF_ROPE], second, sin, ALU.mult))
                nc.gpsimd.tensor_tensor(first, rope_tmp[:, 0, :, 0:HALF_ROPE],
                                        rope_tmp[:, 1, :, 0:HALF_ROPE], ALU.subtract)
                nc.gpsimd.tensor_tensor(second, rope_tmp[:, 0, :, HALF_ROPE:],
                                        rope_tmp[:, 1, :, HALF_ROPE:], ALU.add).then_inc(roped, 1)
                pool.wait_ge(roped, i + 1)

            pool.wait_ge(rope_loaded, 16)
            for i in range(2 * TT):
                rotate(i)
                if i == 2:
                    pool.wait_ge(gm_squared, TT)
                    rstd(rstd_gm, ss_gm, W, gm_rstd)

            def attn_rstd(qt):
                pool.wait_ge(at_squared, qt + 1)
                rstd(rstd_at[:, qt:qt + 1], ss_at[:, qt:qt + 1], W, at_rstd)

            def out_rstd(t):
                pool.wait_ge(o_squared, 2 * t + 2)
                rstd(rstd_o[:, t:t + 1], ss_o[:, 2 * t:2 * t + 1], D, o_rstd,
                     ss_o[:, 2 * t + 1:2 * t + 2])

            def hidden_rstd(t):
                pool.wait_ge(h1_squared, t + 1)
                rstd(rstd_h[:, t:t + 1], ss_h[:, t:t + 1], D, h1_rstd)

            attn_rstd(0)
            attn_rstd(1)
            out_rstd(0)
            hidden_rstd(0)
            attn_rstd(2)
            out_rstd(1)
            hidden_rstd(1)
            attn_rstd(3)
            for t in (2, 3):
                out_rstd(t)
                hidden_rstd(t)
            pool.wait_ge(filled, filled1["ple", 7])
            nc.gpsimd.memset(acc[:], 0.0).then_inc(acc_zeroed, 1)
            for t in range(TT):
                pool.wait_ge(dn_squared, t + 1)
                rstd(rstd_dn[:, t:t + 1], ss_dn[:, t:t + 1], D, dn_rstd)
            for t in range(TT):
                pool.wait_ge(pl_squared, GATE_ORDER.index((t, 1)) + 1)
                rstd(rstd_pl[:, t:t + 1], ss_pl[:, 2 * t:2 * t + 1], D, pl_rstd,
                     ss_pl[:, 2 * t + 1:2 * t + 2])

        @block.sync
        def _(sp):
            sp.dma_start(xT_raw[:, 0], xT[0]).then_inc(xT_loaded[0], 16)
            for k in range(KD):
                sp.dma_start(raw_place(k), weights[k // 2][:, k % 2, :]).then_inc(first_loaded[k], 16)
                if k == 3:
                    sp.dma_start(xT_raw[:, 1], xT[1]).then_inc(xT_loaded[1], 16)
            sp.dma_start(h[:, 0, :], x[0:P]).then_inc(x_loaded[0], 16)
            sp.dma_start(xT_raw[:, 2], xT[2]).then_inc(xT_loaded[2], 16)
            sp.dma_start(h[:, 1, :], x[P:2 * P]).then_inc(x_loaded[1], 16)
            sp.dma_start(xT_raw[:, 3], xT[3]).then_inc(xT_loaded[3], 16)
            for j in range(2):
                sp.dma_start(raw[:, 2 * j:2 * j + 2, :], weights[FIRST_PAIRS + j]).then_inc(raw_loaded[j], 16)
            sp.dma_start(h[:, 2, :], x[2 * P:3 * P]).then_inc(x_loaded[2], 16)
            sp.dma_start(h[:, 3, :], x[3 * P:4 * P]).then_inc(x_loaded[3], 16)
            turns = weights.rearrange("(i j) p k n -> i j p k n", j=2)
            with sp.Fori(FIRST_PAIRS // 2 + 1, PAIRS_OF_SLABS // 2) as i:
                for j in range(2):
                    sp.wait_ge(slab_lo, 4 * i + 2 * j - 2)
                    sp.dma_start(raw[:, 2 * j:2 * j + 2, :],
                                 turns[bass.ds(i, 1), j].rearrange("a p k n -> p (a k) n")
                                 ).then_inc(raw_loaded[j], 16)
            for t in range(TT):
                sp.wait_ge(out_ready, t + 1)
                sp.dma_start(out[t * P:(t + 1) * P, :], h[:, t, :]).then_inc(stored, 16)
            sp.wait_ge(stored, 16 * TT)

        @block.tensor
        def _(pe):
            last_use_pending = [False]

            def product(out, a_hi, a_lo, b_hi, b_lo, first, last):
                begin = nc.tensor.matmul(out, a_hi, b_hi, start=first, stop=False)
                if last_use_pending[0]:
                    begin.then_inc(slab_used, 1)
                    last_use_pending[0] = False
                nc.tensor.matmul(out, a_hi, b_lo, start=False, stop=False)
                return nc.tensor.matmul(out, a_lo, b_hi, start=False, stop=last)

            def bank_free(names, banks, name):
                i = names.index(name)
                users = [n for n in names[:i] if banks[n] == banks[name]]
                if users:
                    pe.wait_ge(*drained[users[-1]])

            def rows_tile(out, k_range, act_hi, act_lo, t, slab, parts, slab_arrives, last_use):
                cut = slice(t * P, (t + 1) * P)
                for k in k_range:
                    if slab_arrives:
                        pe.wait_ge(slab_lo, slab + k + 1)
                    w = ring(slab + k)
                    mm = product(out, act_hi[:, k, cut], act_lo[:, k, cut], w_hi[:, w, :], w_lo[:, w, :],
                                 k == 0, k == parts - 1)
                    last_use_pending[0] = last_use
                    if k == parts - 1:
                        mm.then_inc(filled, 1)

            def proj(n, k_range=range(KD)):
                name = ("proj", n)
                if k_range[0] == 0:
                    bank_free(phase1, bank1, name)
                out = psum[:, bank1[name], :]
                if n < 20:
                    group, t = divmod(n, TT)
                    if k_range[0] == 0 and n < TT:
                        pe.wait_ge(xT_lo_done, t + 1)
                    rows_tile(out, k_range, actT_hi, actT_lo, t, group * KD, KD, t == 0, t == TT - 1)
                    return
                t, half = divmod(n - 20, HALVES)
                if t == 0 and half == 0 and k_range[0] == 0:
                    pe.wait_ge(*drained["gateT", TT - 1])
                if half == 0 and k_range[-1] == KD - 1:
                    pe.wait_ge(*drained["attnT", t])
                rows_tile(out, k_range, mixT_hi, mixT_lo, t, (G_O0 + half) * KD, KD, t == 0, t == TT - 1)

            def turn(names, banks, name, source):
                bank_free(names, banks, name)
                for j in range(4):
                    mm = nc.tensor.transpose(psum[:, banks[name], j * P:(j + 1) * P],
                                             source[:, j * P:(j + 1) * P], ident[:])
                mm.then_inc(filled, 1)

            def mix(i):
                name = ("mix", i)
                bank_free(phase1, bank1, name)
                if i == 0:
                    pe.wait_ge(ws_masked, 1)
                    pe.wait_ge(vn_ready, TT)
                for a in range(2):
                    g = 2 * i + a
                    out = psum[:, bank1[name], a * 256:(a + 1) * 256].rearrange("p (t d) -> p t d", d=GD)
                    mm = nc.tensor.matmul(out, wsT[:, g, :], gv[:, :, g * GD:(g + 1) * GD],
                                          start=True, stop=True)
                mm.then_inc(filled, 1)

            def turn_qk(i):
                pe.wait_ge(roped, i + 1)
                turn(phase1, bank1, ("qkT", i), work[:, i % 2, :])

            def turn_gate(t):
                pe.wait_ge(gm_scaled, t + 1)
                turn(phase1, bank1, ("gateT", t), u[:, t, :])

            def turn_hn(i):
                t, j = divmod(i, 2)
                pe.wait_ge(hn_ready, t + 1)
                turn(phase1, bank1, ("hT", i), work[:, j, :])

            def turn_attn(qt):
                pe.wait_ge(at_scaled, qt + 1)
                turn(phase1, bank1, ("attnT", qt), attn[:])

            pe.wait_ge(constants_set, 4)
            proj(0)
            for n in range(1, 17):
                if n - 1 in (8, 9):
                    mix(2 * (n - 9))
                    mix(2 * (n - 9) + 1)
                if n - 1 >= 9:
                    turn_qk(n - 10)
                if 12 <= n - 1 <= 15:
                    turn_gate(n - 13)
                proj(n)
            turn_qk(7)

            def scores(unit):
                qt, pair = divmod(unit, PAIRS)
                n = (qt + 1) * P
                if pair == 0:
                    pe.wait_ge(*drained["qkT", TT + qt])
                if unit >= 1:
                    pe.wait_ge(probs_ready, unit)
                for s in range(2):
                    part = slice(s * DH, (s + 1) * DH)
                    nc.tensor.matmul(psum[:, BANK_S + s, 0:n], qT[part, pair, qt * P:n],
                                     kT[part, pair, 0:n], start=True, stop=False)
                for s in range(2):
                    mm = nc.tensor.matmul(psum[:, BANK_S + s, n - P:n], ident_bf[:], causal_bf[:],
                                          start=False, stop=True)
                mm.then_inc(scores_ready, 1)

            def turn_probs(unit):
                qt = unit // PAIRS
                pe.wait_ge(probs_ready, unit + 1)
                if unit in (5, 9, 13):
                    pe.wait_ge(*drained["attnT", unit // PAIRS - 1])
                if unit == 14:
                    pe.wait_ge(*drained["hT", 1])
                for s in range(2):
                    for k in range(qt + 1):
                        mm = nc.tensor.transpose(psum[:, BANK_PT + s, k * P:(k + 1) * P],
                                                 probs[:, unit % 2, s, k * P:(k + 1) * P], ident[:])
                    mm.then_inc(pt_filled, 1)

            def attend(unit):
                qt, pair = divmod(unit, PAIRS)
                if pair == 0:
                    pe.wait_ge(act_drained, 16 + qt + 1)
                    if qt:
                        pe.wait_ge(attn_ready, qt)
                for s in range(2):
                    head = 2 * pair + s
                    pe.wait_ge((pt0_drained, pt1_drained)[s], unit + 1)
                    for k in range(qt + 1):
                        mm = nc.tensor.matmul(psum[:, BANK_O, head * DH:(head + 1) * DH],
                                              probsT[:, s, k, :], v[:, k, head * DH:(head + 1) * DH],
                                              start=(k == 0), stop=(k == qt))
                mm.then_inc(pv_done, 1)

            for step in range(TT * PAIRS):
                scores(step)
                if step >= 1:
                    turn_probs(step - 1)
                n, k0 = STEP_TILES[step]
                proj(n, range(k0, k0 + 4))
                if step >= 1:
                    attend(step - 1)
                if step in (5, 9, 13):
                    turn_attn(step // 4 - 1)
                if step == 14:
                    turn_hn(0)
                    turn_hn(1)
            turn_probs(15)
            proj(25, range(0, 4))
            attend(15)
            proj(25, range(4, 8))
            turn_hn(2)
            turn_hn(3)
            proj(26, range(0, 4))
            turn_attn(3)
            proj(26, range(4, 8))
            proj(27)

            def ple_tile(i):
                half, t = divmod(i, TT)
                name = ("ple", i)
                bank_free(phase1, bank1, name)
                if i == 0:
                    pe.wait_ge(pT_lo_done, 1)
                rows_tile(psum[:, bank1[name], :], range(KP), pT_hi, pT_lo, t, SLAB_PLE + half * KP, KP,
                          t == 0, t == TT - 1)

            for i in range(3):
                ple_tile(i)
            turn_hn(4)
            turn_hn(5)
            for i in range(3, 8):
                ple_tile(i)
            turn_hn(6)
            turn_hn(7)
            before_mlp = drained["before_mlp"][1]
            pe.wait_ge(dve_drained, before_mlp)

            def mlp_tiles(c, tiles, fill=True):
                for m in tiles:
                    i, j = divmod(m, TT)
                    out = psum[:, (m + 1) % 8, :]
                    if m != 0:
                        pe.wait_ge(dve_drained, before_mlp + max(m - 7, 0) + 16 * c)
                    for k in range(KD):
                        if j == 0:
                            pe.wait_ge(slab_lo, SLAB_FF + KD * i + k + 1 + SLABS_PER_CHUNK * c)
                        if m == 8:
                            pe.wait_ge(dve_drained, before_mlp + k + 1 + 16 * c)
                        w = i % 2 * KD + k
                        if m < 8:
                            cut = slice(j * P, (j + 1) * P)
                            mm = product(out, w_hi[:, w, cut], w_lo[:, w, cut], actT_hi[:, k, :],
                                         actT_lo[:, k, :], k == 0, k == KD - 1)
                        else:
                            cut = slice(j * P, (j + 1) * P)
                            mm = product(out, mixT_hi[:, k, cut], mixT_lo[:, k, cut], w_hi[:, w, :],
                                         w_lo[:, w, :], k == 0, k == KD - 1)
                        last_use_pending[0] = j == TT - 1
                    mm.then_inc(filled, 1)

            with pe.Fori(0, CHUNKS - 1) as c:
                mlp_tiles(c, range(16))
            last = CHUNKS - 1
            mlp_tiles(last, range(15))

            def turn_h2(i):
                t, j = divmod(i, 2)
                pe.wait_ge(h2_ready, t + 1)
                turn(tail, bank2, ("h2T", i), h[:, t, j * W:(j + 1) * W])

            def gate_tile(t, half):
                name = ("gate", t, half)
                bank_free(tail, bank2, name)
                if half == 0:
                    pe.wait_ge(*drained["h2T", 2 * t + 1])
                rows_tile(psum[:, bank2[name], :], range(KD), actT_hi, actT_lo, t, SLAB_GATE + half * KD,
                          KD, t == 0, False)

            turn_h2(0)
            turn_h2(1)
            mlp_tiles(last, (15,))
            turn_h2(2)
            turn_h2(3)
            gate_tile(0, 0)
            turn_h2(4)
            turn_h2(5)
            gate_tile(1, 0)
            turn_h2(6)
            turn_h2(7)
            for t, half in GATE_ORDER[2:]:
                gate_tile(t, half)


def slab_pairs(w):
    rows, columns = w.shape
    w = w.reshape(rows // 256, 2, P, columns // W, W).transpose(3, 0, 2, 1, 4)
    return w.reshape(-1, P, 2, W)


def kernel(**inputs):
    import numpy as _np
    import concourse.bacc as _bacc
    from concourse import mybir as _mybir
    from concourse.bass_utils import run_bass_kernel_spmd as _run

    a = {name: _np.asarray(value)[0] for name, value in inputs.items()}
    w_in, w_o, w_up, w_down = a["w_in"], a["w_o"], a["w_up"], a["w_down"]
    piece = [w_in[:, i * W:(i + 1) * W] for i in range(5)]
    stream = [slab_pairs(piece[i]) for i in (4, 3, 0, 1, 2)]
    stream.append(slab_pairs(_np.concatenate([w_o[W:], w_o[:W]])))
    stream.append(slab_pairs(a["w_ple"]))
    for c in range(CHUNKS):
        stream += [slab_pairs(w_up[:, c * D:(c + 1) * D]), slab_pairs(w_down[c * D:(c + 1) * D])]
    stream.append(slab_pairs(a["w_ple_gate"]))
    x = a["x"]
    angle_rate = _np.float32(500000.0) ** (-_np.arange(HALF_ROPE, dtype=_np.float32) / _np.float32(HALF_ROPE))
    angle = _np.arange(SEQ, dtype=_np.float32)[:, None] * angle_rate[None, :].astype(_np.float32)
    cos, sin = _np.cos(angle), _np.sin(angle)
    rope = _np.stack([_np.concatenate([cos, cos], 1), _np.concatenate([sin, sin], 1)], 1)
    as_columns = lambda g: g.reshape(-1, P).T
    arrays = {
        "x": x,
        "xT": x.reshape(TT, P, KD, P).transpose(0, 3, 2, 1),
        "pT": a["p"][0].reshape(SEQ, KP, P).transpose(2, 1, 0),
        "weights": _np.concatenate(stream),
        "columns": _np.concatenate([as_columns(a["mix_pre_g"]), as_columns(a["mlp_pre_g"]),
                                    as_columns(a["gmlp_out_g"]), as_columns(a["attn_out_g"]),
                                    a["b_s"].T], 1),
        "rope": rope.reshape(TT, P, 2, 2 * HALF_ROPE).transpose(1, 0, 2, 3).astype(_np.float32),
        "ws": a["w_s"].transpose(2, 0, 1),
        "row_ln": _np.stack([a["gmlp_ln_g"], a["gmlp_ln_b"]])[None],
        "row_mix_post": a["mix_post_g"][None],
        "row_mlp_post": a["mlp_post_g"][None],
        "row_gate": _np.stack([a["b_ple_gate"], a["ple_post_g"]])[None],
    }
    nc = _bacc.Bacc("TRN2", target_bir_lowering=False, num_devices=1)
    aps, fed = {}, {}
    for name, value in arrays.items():
        fed[name + "_dram"] = _np.ascontiguousarray(value)
        aps[name] = nc.dram_tensor(name + "_dram", value.shape, _mybir.dt.float32, kind="ExternalInput").ap()
    out = nc.dram_tensor("out_dram", (SEQ, D), _mybir.dt.float32, kind="ExternalOutput").ap()
    rows = {name[4:]: ap.to_broadcast([P, *ap.shape[1:]]) for name, ap in aps.items()
            if name.startswith("row_")}
    hymba_layer(nc, aps["x"], aps["xT"], aps["pT"], aps["weights"], aps["columns"], aps["rope"],
                aps["ws"], rows, out)
    result = _run(nc, [fed], core_ids=[0])
    return result.results[0]["out_dram"].reshape(1, SEQ, D)
```

```python
from contextlib import ExitStack

import concourse.bass as bass
from concourse import mybir

F32 = mybir.dt.float32
F32R = mybir.dt.float32r
BF16 = mybir.dt.bfloat16
ALU = mybir.AluOpType
ACT = mybir.ActivationFunctionType
AXIS_X = mybir.AxisListType.X

P = 128
D = 1024
SEQ = 512
TT = SEQ // P
KD = D // P
W = 512
HALVES = D // W
HEADS, DH = 8, 64
PAIRS = HEADS // 2
GROUPS, GD = 8, 64
D_PLE = 256
KP = D_PLE // P
D_FF = 4 * D
CHUNKS = D_FF // D
HALF_ROPE = DH // 4 // 2
EPS = 1e-6
NEG = -1e30
KIB = 1024
SCALE = DH ** -0.5

G_GV, G_U, G_Q, G_K, G_V, G_O0, G_O1, G_PLE, G_FF = range(9)
SLAB_PLE = 7 * KD
SLAB_FF = SLAB_PLE + HALVES * KP
SLABS_PER_CHUNK = 4 * KD
SLAB_GATE = SLAB_FF + CHUNKS * SLABS_PER_CHUNK
SLABS = SLAB_GATE + HALVES * KD
PAIRS_OF_SLABS = SLABS // 2
FIRST_PAIRS = KD // 2

WARM_UP_MATMULS = 42

BANK_S, BANK_PT, BANK_O = 3, 5, 7


def phase_one_results():
    names = []
    for n in range(20):
        names.append(("proj", n))
        if n in (8, 9):
            names += [("mix", 2 * (n - 8)), ("mix", 2 * (n - 8) + 1)]
        if 9 <= n <= 16:
            names.append(("qkT", n - 9))
        if 12 <= n <= 15:
            names.append(("gateT", n - 12))
    names += [("proj", n) for n in range(20, 26)]
    first = {"proj": 0, "mix": BANK_S, "qkT": BANK_PT, "gateT": BANK_O}
    turns = {"proj": 3, "mix": 2, "qkT": 2, "gateT": 1}
    banks = {(kind, i): first[kind] + i % turns[kind] for kind, i in names}
    banks["proj", 3], banks["proj", 4], banks["proj", 5] = BANK_S, BANK_S + 1, BANK_PT
    a, b, c = (banks["proj", n] for n in (20, 21, 22))
    late = [(("attnT", 0), b), (("proj", 20), a), (("proj", 21), b), (("attnT", 1), c),
            (("proj", 22), c), (("proj", 23), a), (("attnT", 2), b), (("proj", 24), b),
            (("hT", 0), 5), (("hT", 1), 6), (("proj", 25), c), (("hT", 2), a), (("hT", 3), 6),
            (("attnT", 3), 5), (("proj", 26), 3), (("proj", 27), 4),
            (("ple", 0), 7), (("ple", 1), 6), (("ple", 2), 5), (("hT", 4), a), (("hT", 5), b),
            (("ple", 3), c), (("ple", 4), 7), (("ple", 5), 6), (("hT", 6), 3),
            (("hT", 7), 4), (("ple", 6), 5), (("ple", 7), a)]
    banks.update(late)
    return names[:-6] + [name for name, _ in late], banks


def tail_results():
    late = [(("down", 0), 5), (("down", 1), 6), (("down", 2), 7), (("h2T", 0), 1), (("h2T", 1), 2),
            (("down", 3), 0), (("h2T", 2), 3), (("h2T", 3), 4), (("gate", 0), 5),
            (("h2T", 4), 6), (("h2T", 5), 7), (("gate", 1), 0), (("h2T", 6), 1), (("h2T", 7), 2)]
    late += [(("gate", i), (i + 1) % 8) for i in range(2, len(GATE_TILES))]
    return [name for name, _ in late], dict(late)


X_PIECES = ((0, range(0, 4)), (1, range(0, 4)), (0, range(4, 8)), (1, range(4, 8)),
            (2, range(KD)), (3, range(KD)))
FIRST_ORDER = ("x0", 0, 1, 2, "x1", 3, "x2", 4, 5, "x3", 6, 7, "x4", "x5")
GATE_TILES = ((0, 0, W), (1, 0, W), (0, W, W), (1, W, W), (2, 0, W), (2, W, W), (3, 0, W),
              (3, W, W // 2), (3, W + W // 2, W // 2))


def gate_tiles_of(t):
    return [i for i, tile in enumerate(GATE_TILES) if tile[0] == t]


STEP_TILES = [(17, 0), (17, 4), (18, 0), (18, 4), (19, 0), (19, 4), (20, 0), (20, 4),
              (21, 0), (21, 4), (22, 0), (22, 4), (23, 0), (23, 4), (24, 0), (24, 4)]
STEP_SPLITS = {0: [G_O0 * KD + 2], 1: [G_O0 * KD + 4], 2: [G_O0 * KD + 6], 5: [G_O1 * KD],
               6: [G_O1 * KD + 2], 7: [G_O1 * KD + 4], 8: [G_O1 * KD + 6]}


def hymba_layer(nc, x, xT, pT, weights, columns, rope, ws, rows, out):
    phase1, bank1 = phase_one_results()
    tail, bank2 = tail_results()
    filled1 = {name: i + 1 for i, name in enumerate(phase1)}
    FILLED_FF = len(phase1)
    filled2 = {name: FILLED_FF + 16 * (CHUNKS - 1) + 12 + i + 1 for i, name in enumerate(tail)}

    with ExitStack() as ctx:
        top = [0]

        def place(name, shape, dt=F32, at=None):
            size = 2 if dt == BF16 else 4
            for n in shape[1:]:
                size *= n
            if at is None:
                at = top[0]
                top[0] += -(-size // 32) * 32
            return nc.alloc_sbuf_tensor_at(name, shape, dt, offset=at)

        base = nc.sbuf_base
        top[0] = -(-base // 32) * 32
        h = place("h", [P, TT, D])
        actT_hi = place("actT_hi", [P, KD, SEQ], F32R)
        actT_lo = place("actT_lo", [P, KD, SEQ], F32R)
        at_mixed_hi = top[0]
        mixT_hi = place("mixT_hi", [P, KD, SEQ], F32R)
        at_mixed_lo = top[0]
        mixT_lo = place("mixT_lo", [P, KD, SEQ], F32R)
        w_hi = place("w_hi", [P, 2 * KD, W], F32R)
        w_lo = place("w_lo", [P, 2 * KD, W], F32R)
        raw = place("raw", [P, 4, W])
        gain_post = place("gain_post", [P, D])
        work = place("work", [P, 2, W])
        junk = place("junk", [P, D])
        cols = place("cols", [P, columns.shape[1]])
        rope_sb = place("rope_sb", [P, TT, 2, 2 * HALF_ROPE])
        rope_tmp = place("rope_tmp", [P, 2, HEADS, 2 * HALF_ROPE])
        rinv = place("rinv", [P, HEADS])
        ident = place("ident", [P, P])
        ident_bf = place("ident_bf", [P, P], BF16)
        causal = place("causal", [P, P])
        stat = place("stat", [P, 114 + len(GATE_TILES)])
        rowsum = place("rowsum", [P, TT * PAIRS, 2])
        at_area = top[0]
        kT_hi = place("kT_hi", [P, PAIRS, SEQ], F32R)
        kT_lo = place("kT_lo", [P, PAIRS, SEQ], F32R)
        v = place("v", [P, TT, W])
        probs = place("probs", [P, 2, 2, SEQ])
        probsT = place("probsT", [P, 2, TT, P])
        attn = place("attn", [P, W])
        assert top[0] <= nc.sbuf_usable_end
        qT_hi, qT_lo = mixT_hi[:, PAIRS:2 * PAIRS, :], mixT_lo[:, PAIRS:2 * PAIRS, :]
        xT_raw = place("xT_raw", [P, TT, KD, P], at=at_area)
        u = place("u", [P, TT, W], at=at_area + 24 * KIB)
        ln_gb = place("ln_gb", [P, 2, W], at=at_area + 32 * KIB)
        first_raw = [place("first_raw_a", [P, KD // 2, W], at=at_mixed_hi),
                     place("first_raw_b", [P, KD // 2, W], at=at_mixed_lo)]
        gv = place("gv", [P, TT, W], at=at_mixed_hi + 8 * KIB)
        wsT = place("wsT", [P, GROUPS, P], at=at_mixed_lo + 8 * KIB)
        ple = place("ple", [P, TT, D], at=at_area)
        acc = place("acc", [P, TT, D], at=at_area + 16 * KIB)
        pT_raw = place("pT_raw", [P, KP, SEQ], at=at_area + 16 * KIB)
        pT_hi = place("pT_hi", [P, KP, SEQ], F32R, at=at_area + 20 * KIB)
        pT_lo = place("pT_lo", [P, KP, SEQ], F32R, at=at_area + 24 * KIB)
        gate_rows = place("gate_rows", [P, 2, D], at=at_mixed_hi)

        psum = ctx.enter_context(nc.psum_tensor("psum", [P, 8, W], F32))

        mix_pre = lambda k: cols[:, k:k + 1]
        mlp_pre = lambda k: cols[:, 8 + k:9 + k]
        mixed_gain = lambda k: cols[:, 16 + k:17 + k]
        b_s = lambda g: cols[:, 24 + g:25 + g]
        minus_half = stat[:, 0:4]
        ss_x, rstd_x = stat[:, 4:8], stat[:, 8:12]
        ss_gm, rstd_gm = stat[:, 12:16], stat[:, 16:20]
        ss_at, rstd_at = stat[:, 20:24], stat[:, 24:28]
        ss_o, rstd_o = stat[:, 28:36], stat[:, 36:40]
        ss_h, rstd_h = stat[:, 40:44], stat[:, 44:48]
        ss_dn, rstd_dn = stat[:, 48:52], stat[:, 52:56]
        ss_pl, rstd_pl = stat[:, 114:], stat[:, 64:68]
        ple_tmp = stat[:, 56:59]
        pool_tmp = stat[:, 68:72]
        mean_var = stat[:, 72:80].rearrange("p (t c) -> p t c", c=2)
        rstd_ln = stat[:, 80:84]
        bn6 = lambda t: stat[:, 90 + 6 * t:96 + 6 * t]
        table_loaded = stat[:, 88:89]
        neg_max = stat[:, 84:86]
        row_max = stat[:, 86:88]

        def sem(name):
            return ctx.enter_context(nc.semaphore(name))

        xT_loaded = [sem(f"xT_loaded{i}") for i in range(len(X_PIECES))]
        x_loaded = [sem(f"x_loaded{t}") for t in range(TT)]
        first_loaded = [sem(f"first_loaded{k}") for k in range(KD)]
        raw_loaded = [sem(f"raw_loaded{j}") for j in range(2)]
        cols_loaded, rope_loaded, ws_loaded = sem("cols_loaded"), sem("rope_loaded"), sem("ws_loaded")
        ln_loaded, post_loaded, pT_loaded = sem("ln_loaded"), sem("post_loaded"), sem("pT_loaded")
        gate_rows_loaded, stored = sem("gate_rows_loaded"), sem("stored")
        slab_hi, slab_lo, slab_used = sem("slab_hi"), sem("slab_lo"), sem("slab_used")
        filled, act_drained, dve_drained = sem("filled"), sem("act_drained"), sem("dve_drained")
        constants_set, ws_masked, acc_zeroed = sem("constants_set"), sem("ws_masked"), sem("acc_zeroed")
        xT_hi_done, xT_lo_done, x_squared, x_rstd = (sem("xT_hi_done"), sem("xT_lo_done"),
                                                     sem("x_squared"), sem("x_rstd"))
        ln_stats, ln_mean, ln_rstd, ln_centred, vn_ready = (sem("ln_stats"), sem("ln_mean"),
                                                            sem("ln_rstd"), sem("ln_centred"),
                                                            sem("vn_ready"))
        roped = sem("roped")
        gm_squared, gm_rstd, gm_scaled = sem("gm_squared"), sem("gm_rstd"), sem("gm_scaled")
        turned_hi = sem("turned_hi")
        scores_masked = sem("scores_masked")
        scores_ready, max_found, max_ready, probs_ready = (sem("scores_ready"), sem("max_found"),
                                                           sem("max_ready"), sem("probs_ready"))
        pt_filled, pt0_drained, pt1_drained, pv_done = (sem("pt_filled"), sem("pt0_drained"),
                                                        sem("pt1_drained"), sem("pv_done"))
        rinv_ready, attn_ready, at_squared, at_rstd, at_scaled = (
            sem("rinv_ready"), sem("attn_ready"), sem("at_squared"), sem("at_rstd"), sem("at_scaled"))
        o_squared, o_rstd, o_normed = sem("o_squared"), sem("o_rstd"), sem("o_normed")
        h1_squared, h1_rstd, hn_ready = sem("h1_squared"), sem("h1_rstd"), sem("hn_ready")
        pT_hi_done, pT_lo_done = sem("pT_hi_done"), sem("pT_lo_done")
        relu_done, ff_squared, ff_hi_done = sem("relu_done"), sem("ff_squared"), sem("ff_hi_done")
        dn_squared, dn_rstd, dn_normed, h2_ready = (sem("dn_squared"), sem("dn_rstd"),
                                                    sem("dn_normed"), sem("h2_ready"))
        sig_done, pl_gated, pl_squared, pl_rstd, pl_gained, out_ready = (
            sem("sig_done"), sem("pl_gated"), sem("pl_squared"), sem("pl_rstd"),
            sem("pl_gained"), sem("out_ready"))
        pool_chain = sem("pool_chain")

        def ring(slab):
            if slab < SLAB_PLE:
                return (slab // KD % 2) * KD + slab % KD
            if slab < SLAB_FF:
                return KD + slab - SLAB_PLE
            return ((slab - SLAB_FF) // KD % 2) * KD + (slab - SLAB_FF) % KD

        def gain_of(slab):
            if slab < G_O0 * KD:
                return mix_pre(slab % KD)
            if slab < SLAB_PLE:
                return mixed_gain(slab % KD)
            i = (slab - SLAB_FF) % SLABS_PER_CHUNK
            if SLAB_FF <= slab < SLAB_GATE and i < 2 * KD:
                return mlp_pre(i % KD)
            return None

        def raw_place(slab):
            if slab < KD:
                return first_raw[slab // 4][:, slab % 4, :]
            return raw[:, slab % 4, :]

        drained = {}

        block = ctx.enter_context(nc.Block())

        @block.vector
        def _(dve):
            count = [0]

            def drained_by_dve(instruction, name):
                instruction.then_inc(dve_drained, 1)
                count[0] += 1
                drained[name] = (dve_drained, count[0])

            def split_lo(gain, source, place_at):
                high = w_hi[:, place_at, :].bitcast(F32)
                if gain is None:
                    nc.vector.tensor_tensor(w_lo[:, place_at, :], source, high, ALU.subtract
                                            ).then_inc(slab_lo, 1)
                else:
                    nc.vector.scalar_tensor_tensor(out=w_lo[:, place_at, :], in0=source, scalar=gain,
                                                   in1=high, op0=ALU.mult, op1=ALU.subtract
                                                   ).then_inc(slab_lo, 1)

            def splits(slab):
                for s in (slab, slab + 1):
                    dve.wait_ge(slab_hi, s + 1)
                    split_lo(gain_of(s), raw_place(s), ring(s))

            turned = [0]

            def turn_lo(name, target, high, bank):
                turned[0] += 1
                dve.wait_ge(turned_hi, turned[0])
                drained_by_dve(nc.vector.tensor_tensor(
                    target, psum[:, bank, :].rearrange("p (k n) -> p k n", n=P),
                    high.bitcast(F32), ALU.subtract), name)

            def xT_lo(i):
                t, ks = X_PIECES[i]
                dve.wait_ge(xT_hi_done, i + 1)
                part, cut = slice(ks[0], ks[-1] + 1), slice(t * P, (t + 1) * P)
                nc.vector.tensor_tensor(actT_lo[:, part, cut], xT_raw[:, t, part],
                                        actT_hi[:, part, cut].bitcast(F32), ALU.subtract
                                        ).then_inc(xT_lo_done, 1)

            for item in FIRST_ORDER:
                if isinstance(item, str):
                    xT_lo(int(item[1]))
                else:
                    dve.wait_ge(slab_hi, item + 1)
                    split_lo(gain_of(item), raw_place(item), item)
            splits(KD)
            splits(KD + 2)

            def ln_stats_of(t):
                dve.wait_ge(act_drained, t + 1)
                nc.vector.bn_stats(bn6(t), gv[:, t, :]).then_inc(ln_stats, 1)
                dve.wait_ge(ln_stats, t + 1)
                nc.vector.bn_aggr(mean_var[:, t, :], bn6(t)).then_inc(ln_mean, 1)

            def ln_centre(t):
                dve.wait_ge(ln_rstd, t + 1)
                nc.vector.tensor_scalar(gv[:, t, :], gv[:, t, :], mean_var[:, t, 0:1],
                                        rstd_ln[:, t:t + 1], ALU.subtract, ALU.mult
                                        ).then_inc(ln_centred, 1)

            def mix_drain(i):
                bank = psum[:, bank1["mix", i], :]
                dve.wait_ge(filled, filled1["mix", i])
                if i == 0:
                    dve.wait_ge(act_drained, 2 * TT)
                for a in range(2):
                    g = 2 * i + a
                    part = u[:, :, g * GD:(g + 1) * GD]
                    last = nc.vector.scalar_tensor_tensor(
                        out=part, in0=bank[:, a * 256:(a + 1) * 256].rearrange("p (t d) -> p t d", d=GD),
                        scalar=b_s(g), in1=part, op0=ALU.add, op1=ALU.mult)
                drained_by_dve(last, ("mix", i))

            def qkT_lo(i):
                cut = slice(i % TT * P, (i % TT + 1) * P)
                high, low = ((qT_hi, qT_lo), (kT_hi, kT_lo))[i // TT]
                if i == TT:
                    dve.wait_ge(xT_lo_done, len(X_PIECES))
                turn_lo(("qkT", i), low[:, :, cut], high[:, :, cut], bank1["qkT", i])

            def gate_turn_lo(t):
                cut = slice(t * P, (t + 1) * P)
                turn_lo(("gateT", t), mixT_lo[:, 0:4, cut], mixT_hi[:, 0:4, cut], bank1["gateT", t])

            for n in range(16):
                if n:
                    splits(KD + 2 * (n + 1))
                if n < TT:
                    ln_stats_of(n)
                if 2 <= n <= TT + 1:
                    ln_centre(n - 2)
                if n in (9, 10):
                    mix_drain(2 * (n - 9))
                    mix_drain(2 * (n - 9) + 1)
                if n >= 10:
                    qkT_lo(n - 10)
                if n == 11:
                    dve.wait_ge(gm_rstd, 1)
                    for t in range(TT):
                        nc.vector.tensor_scalar(u[:, t, :], u[:, t, :], rstd_gm[:, t:t + 1], None,
                                                ALU.mult).then_inc(gm_scaled, 1)
                if 12 <= n <= 15:
                    gate_turn_lo(n - 12)
            qkT_lo(6)
            qkT_lo(7)

            def row_maxima(unit):
                n = (unit // PAIRS + 1) * P
                dve.wait_ge(scores_ready, unit + 1)
                diagonal = psum[:, BANK_S:BANK_S + 2, n - P:n]
                nc.vector.tensor_tensor(diagonal, diagonal, causal[:, None, :].to_broadcast([P, 2, P]),
                                        ALU.add).then_inc(scores_masked, 1)
                dve.wait_ge(scores_masked, unit + 1)
                if unit >= 1:
                    dve.wait_ge(probs_ready, unit)
                nc.vector.tensor_reduce(row_max, psum[:, BANK_S:BANK_S + 2, 0:n], AXIS_X, ALU.max
                                        ).then_inc(max_found, 1)
                dve.wait_ge(max_found, unit + 1)
                nc.vector.tensor_scalar(neg_max, row_max, -SCALE, None, ALU.mult).then_inc(max_ready, 1)

            def drain_pt0(unit):
                n = (unit // PAIRS + 1) * P
                dve.wait_ge(pt_filled, 2 * unit + 1)
                nc.vector.tensor_copy(probsT[:, 0].rearrange("p k q -> p (k q)")[:, 0:n],
                                      psum[:, BANK_PT, 0:n]).then_inc(pt0_drained, 1)

            def attn_rows(qt):
                dve.wait_ge(pv_done, PAIRS * (qt + 1))
                sums = rowsum[:, PAIRS * qt:PAIRS * (qt + 1), :].rearrange("p a b -> p (a b)")
                nc.vector.reciprocal(rinv[:], sums).then_inc(rinv_ready, 1)
                dve.wait_ge(rinv_ready, qt + 1)
                nc.vector.tensor_tensor(attn[:].rearrange("p (h d) -> p h d", d=DH),
                                        psum[:, BANK_O, :].rearrange("p (h d) -> p h d", d=DH),
                                        rinv[:, :, None].to_broadcast([P, HEADS, DH]), ALU.mult
                                        ).then_inc(attn_ready, 1)

            def attn_scale(qt):
                dve.wait_ge(at_rstd, qt + 1)
                nc.vector.tensor_scalar(attn[:], attn[:], rstd_at[:, qt:qt + 1], None, ALU.mult
                                        ).then_inc(at_scaled, 1)

            def attn_turn_lo(qt):
                cut = slice(qt * P, (qt + 1) * P)
                turn_lo(("attnT", qt), mixT_lo[:, 4:8, cut], mixT_hi[:, 4:8, cut], bank1["attnT", qt])

            def add_mixed(t):
                if t == 0:
                    dve.wait_ge(post_loaded, 16)
                dve.wait_ge(o_rstd, t + 1)
                for half in range(HALVES):
                    n = 20 + 2 * t + half
                    bank = psum[:, bank1["proj", n], :]
                    cut = slice(half * W, (half + 1) * W)
                    nc.vector.scalar_tensor_tensor(out=bank, in0=bank, scalar=rstd_o[:, t:t + 1],
                                                   in1=gain_post[:, cut], op0=ALU.mult, op1=ALU.mult
                                                   ).then_inc(o_normed, 1)
                for half in range(HALVES):
                    n = 20 + 2 * t + half
                    bank = psum[:, bank1["proj", n], :]
                    cut = slice(half * W, (half + 1) * W)
                    dve.wait_ge(o_normed, 2 * t + half + 1)
                    drained_by_dve(nc.vector.tensor_tensor(h[:, t, cut], h[:, t, cut], bank, ALU.add),
                                   ("proj", n))

            def hn_turn_lo(i):
                t, j = divmod(i, 2)
                cut = slice(t * P, (t + 1) * P)
                turn_lo(("hT", i), actT_lo[:, 4 * j:4 * j + 4, cut], actT_hi[:, 4 * j:4 * j + 4, cut],
                        bank1["hT", i])

            for step in range(TT * PAIRS):
                if step >= 6 and step % 4 == 2:
                    attn_turn_lo(step // 4 - 1)
                row_maxima(step)
                if step >= 1:
                    drain_pt0(step - 1)
                if step >= 5 and step % 4 == 1:
                    attn_scale(step // 4 - 1)
                for slab in STEP_SPLITS.get(step, ()):
                    splits(slab)
                if step >= 4 and step % 4 == 0:
                    attn_rows(step // 4 - 1)
                if step == 11:
                    add_mixed(0)
                if step == 15:
                    add_mixed(1)
            drain_pt0(15)
            hn_turn_lo(0)
            hn_turn_lo(1)
            attn_rows(3)
            attn_scale(3)
            hn_turn_lo(2)
            hn_turn_lo(3)
            attn_turn_lo(3)
            for i in range(2):
                splits(SLAB_PLE + 2 * i)
            add_mixed(2)
            dve.wait_ge(pT_hi_done, 1)
            nc.vector.tensor_tensor(pT_lo[:], pT_raw[:], pT_hi[:].bitcast(F32), ALU.subtract
                                    ).then_inc(pT_lo_done, 1)
            splits(SLAB_FF)

            def ple_drain(i):
                half, t = divmod(i, TT)
                dve.wait_ge(filled, filled1["ple", i])
                drained_by_dve(nc.vector.tensor_copy(ple[:, t, half * W:(half + 1) * W],
                                                     psum[:, bank1["ple", i], :]), ("ple", i))

            ple_drain(0)
            add_mixed(3)
            ple_drain(1)
            splits(SLAB_FF + 2)
            ple_drain(2)
            hn_turn_lo(4)
            hn_turn_lo(5)
            ple_drain(3)
            ple_drain(4)
            hn_turn_lo(6)
            hn_turn_lo(7)
            splits(SLAB_FF + 4)
            splits(SLAB_FF + 6)
            for i in range(5, 8):
                ple_drain(i)
            before_mlp = count[0]
            drained["before_mlp"] = (dve_drained, before_mlp)

            def mlp_tiles(c, tiles, gate_next=False):
                for m in tiles:
                    i, j = divmod(m, TT)
                    off = KD * (i + 1) + 2 * j
                    s = SLAB_FF + off
                    place_at = ((i + 1) % 2) * KD + 2 * j
                    gain = [mlp_pre(2 * j + a) if i in (0, 3) else None for a in range(2)]
                    if gate_next:
                        gain = [None, None]
                    bank = psum[:, (m + 1) % 8, :]

                    def lo(a):
                        dve.wait_ge(slab_hi, s + a + 1 + SLABS_PER_CHUNK * c)
                        split_lo(gain[a], raw[:, (s + a) % 4, :], place_at + a)

                    lo(0)
                    if m < 8:
                        dve.wait_ge(relu_done, m + 1 + 8 * c)
                        nc.vector.scalar_tensor_tensor(out=bank, in0=bank, scalar=0.0,
                                                       in1=work[:, m % 2, :], op0=ALU.max, op1=ALU.mult
                                                       ).then_inc(ff_squared, 1)
                        lo(1)
                        dve.wait_ge(ff_hi_done, m + 1 + 8 * c)
                        nc.vector.tensor_tensor(mixT_lo[:, m, :], bank, mixT_hi[:, m, :].bitcast(F32),
                                                ALU.subtract).then_inc(dve_drained, 1)
                        continue
                    lo(1)
                    half, t = divmod(m - 8, TT)
                    part = acc[:, t, half * W:(half + 1) * W]
                    if m == 8:
                        dve.wait_ge(acc_zeroed, 1)
                    if gate_next:
                        dve.wait_ge(filled, filled2["down", t])
                    else:
                        dve.wait_ge(filled, FILLED_FF + m + 1 + 16 * c)
                    nc.vector.tensor_tensor(part, part, bank, ALU.add).then_inc(dve_drained, 1)

            with dve.Fori(0, CHUNKS - 1) as c:
                mlp_tiles(c, range(16))
            last = CHUNKS - 1
            mlp_tiles(last, range(12))
            count[0] += 16 * CHUNKS - TT

            def add_mlp(t):
                if t == 0:
                    dve.wait_ge(post_loaded, 32)
                dve.wait_ge(dn_rstd, t + 1)
                nc.vector.scalar_tensor_tensor(out=acc[:, t, :], in0=acc[:, t, :],
                                               scalar=rstd_dn[:, t:t + 1], in1=gain_post[:],
                                               op0=ALU.mult, op1=ALU.mult).then_inc(dn_normed, 1)
                dve.wait_ge(dn_normed, t + 1)
                nc.vector.tensor_tensor(h[:, t, :], h[:, t, :], acc[:, t, :], ALU.add
                                        ).then_inc(h2_ready, 1)

            def h2_turn_lo(i):
                t, j = divmod(i, 2)
                cut = slice(t * P, (t + 1) * P)
                turn_lo(("h2T", i), actT_lo[:, 4 * j:4 * j + 4, cut], actT_hi[:, 4 * j:4 * j + 4, cut],
                        bank2["h2T", i])

            def gate_bias(i):
                t, c0, width = GATE_TILES[i]
                cut = slice(c0, c0 + width)
                if i == 0:
                    dve.wait_ge(gate_rows_loaded, 16)
                dve.wait_ge(filled, filled2["gate", i])
                drained_by_dve(nc.vector.tensor_tensor(acc[:, t, cut], psum[:, bank2["gate", i], 0:width],
                                                       gate_rows[:, 0, cut], ALU.add), ("gate", i))

            def gate_ple(i):
                t, c0, width = GATE_TILES[i]
                cut = slice(c0, c0 + width)
                dve.wait_ge(sig_done, i + 1)
                nc.vector.tensor_tensor(acc[:, t, cut], acc[:, t, cut], ple[:, t, cut], ALU.mult
                                        ).then_inc(pl_gated, 1)

            def gain_ple(i):
                t, c0, width = GATE_TILES[i]
                cut = slice(c0, c0 + width)
                dve.wait_ge(pl_gated, i + 1)
                nc.vector.tensor_tensor(ple[:, t, cut], acc[:, t, cut], gate_rows[:, 1, cut], ALU.mult
                                        ).then_inc(pl_gained, 1)

            def add_ple(t, *tiles):
                gain_ple(tiles[-1])
                dve.wait_ge(pl_rstd, t + 1)
                dve.wait_ge(pl_gained, tiles[-1] + 1)
                for i in tiles:
                    cut = slice(GATE_TILES[i][1], GATE_TILES[i][1] + GATE_TILES[i][2])
                    nc.vector.scalar_tensor_tensor(out=h[:, t, cut], in0=ple[:, t, cut],
                                                   scalar=rstd_pl[:, t:t + 1], in1=h[:, t, cut],
                                                   op0=ALU.mult, op1=ALU.add).then_inc(out_ready, 1)

            def tail_down(t):
                mlp_tiles(last, (12 + t,), gate_next=True)
                count[0] += 1
                drained["down", t] = (dve_drained, count[0])

            tail_down(0)
            tail_down(1)
            add_mlp(0)
            tail_down(2)
            add_mlp(1)
            h2_turn_lo(0)
            h2_turn_lo(1)
            tail_down(3)
            add_mlp(2)
            h2_turn_lo(2)
            h2_turn_lo(3)
            splits(SLAB_GATE + KD)
            add_mlp(3)
            h2_turn_lo(4)
            h2_turn_lo(5)
            splits(SLAB_GATE + KD + 2)
            splits(SLAB_GATE + KD + 4)
            h2_turn_lo(6)
            h2_turn_lo(7)
            splits(SLAB_GATE + KD + 6)
            for i, (t, c0, width) in enumerate(GATE_TILES):
                gate_bias(i)
                gate_ple(i)
                if i == gate_tiles_of(t)[-1]:
                    add_ple(t, *gate_tiles_of(t))
                else:
                    gain_ple(i)

        @block.scalar
        def _(act):
            act.dma_start(cols[:], columns).then_inc(cols_loaded, 16)
            act.wait_ge(constants_set, 1)
            nc.scalar.activation(table_loaded, minus_half[:, 0:1], ACT.Copy)

            def split_hi(slab, gain, source, place_at):
                if gain is None:
                    nc.scalar.activation(w_hi[:, place_at, :], source, ACT.Copy).then_inc(slab_hi, 1)
                else:
                    nc.scalar.activation(w_hi[:, place_at, :], source, ACT.Copy,
                                         scale=gain).then_inc(slab_hi, 1)

            def split_hi_pair(slab, free_at):
                pair = slab // 2
                act.wait_ge(raw_loaded[pair % 2], 16 * ((pair - FIRST_PAIRS) // 2 + 1))
                if free_at:
                    act.wait_ge(slab_used, free_at)
                for s in (slab, slab + 1):
                    split_hi(s, gain_of(s), raw_place(s), ring(s))

            def splits(slab):
                split_hi_pair(slab, slab - 14 if slab >= 2 * KD else 0)

            def turn_hi(result, target, bank):
                act.wait_ge(filled, result)
                nc.scalar.activation(target, psum[:, bank, :].rearrange("p (k n) -> p k n", n=P),
                                     ACT.Copy).then_inc(turned_hi, 1)

            junk_written = []
            squares = {}

            def square(source, sums, done):
                if junk_written:
                    act.wait_ge(*junk_written[-1])
                nc.scalar.activation(junk[:, 0:source.shape[-1]], source, ACT.Square,
                                     accum_out=sums).then_inc(done, 1)
                squares[done.name] = squares.get(done.name, 0) + 1
                junk_written.append((done, squares[done.name]))

            def square_x(t):
                act.wait_ge(x_loaded[t], 16)
                square(h[:, t, :], ss_x[:, t:t + 1], x_squared)

            def xT_hi(i):
                t, ks = X_PIECES[i]
                part = slice(ks[0], ks[-1] + 1)
                act.wait_ge(xT_loaded[i], 16)
                nc.scalar.activation(actT_hi[:, part, t * P:(t + 1) * P], xT_raw[:, t, part], ACT.Copy
                                     ).then_inc(xT_hi_done, 1)

            for item in FIRST_ORDER:
                if isinstance(item, str):
                    xT_hi(int(item[1]))
                    continue
                if item == 0:
                    act.wait_ge(cols_loaded, 16)
                act.wait_ge(first_loaded[item], 16)
                split_hi(item, gain_of(item), raw_place(item), item)
                if item == KD - 1:
                    act.dma_start(h[:, 2, :], x[2 * P:3 * P]).then_inc(x_loaded[2], 16)
                    act.dma_start(h[:, 3, :], x[3 * P:4 * P]).then_inc(x_loaded[3], 16)
            square_x(0)
            square_x(1)
            splits(KD)
            splits(KD + 2)

            def proj_drain(n):
                group, t = divmod(n, TT)
                bank = psum[:, bank1["proj", n], :]
                if n < TT:
                    act.wait_ge(x_rstd, t + 1)
                act.wait_ge(filled, filled1["proj", n])
                rstd = rstd_x[:, t:t + 1]
                if group == G_GV:
                    last = nc.scalar.activation(gv[:, t, :], bank, ACT.Gelu, scale=rstd)
                elif group == G_U:
                    if t == 0:
                        act.wait_ge(xT_lo_done, len(X_PIECES))
                    last = nc.scalar.activation(u[:, t, :], bank, ACT.Gelu, scale=rstd)
                elif group in (G_Q, G_K):
                    i = n - 2 * TT
                    if i >= 2:
                        act.wait_ge(filled, filled1["qkT", i - 2])
                    last = nc.scalar.activation(work[:, i % 2, :], bank, ACT.Copy, scale=rstd)
                else:
                    last = nc.scalar.activation(v[:, t, :], bank, ACT.Copy, scale=rstd)
                last.then_inc(act_drained, 1)
                drained["proj", n] = (act_drained, n + 1)

            def qkT_hi(i):
                cut = slice(i % TT * P, (i % TT + 1) * P)
                if i == TT:
                    act.wait_ge(xT_lo_done, len(X_PIECES))
                turn_hi(filled1["qkT", i], (qT_hi, kT_hi)[i // TT][:, :, cut], bank1["qkT", i])

            for n in range(16):
                if n:
                    splits(KD + 2 * (n + 1))
                if n in (0, 1):
                    square_x(n + 2)
                if n == 1:
                    act.dma_start(ln_gb[:], rows["ln"]).then_inc(ln_loaded, 16)
                if n == 4:
                    act.dma_start(wsT[:], ws).then_inc(ws_loaded, 16)
                if n == 6:
                    act.dma_start(rope_sb[:], rope).then_inc(rope_loaded, 16)
                if n == 10:
                    act.dma_start(gain_post[:], rows["mix_post"]).then_inc(post_loaded, 16)
                if n == 10:
                    act.wait_ge(*drained["mix", 3])
                    for t in range(TT):
                        square(u[:, t, :], ss_gm[:, t:t + 1], gm_squared)
                if n >= 10:
                    qkT_hi(n - 10)
                proj_drain(n)
                if 12 <= n <= 15:
                    t = n - 12
                    turn_hi(filled1["gateT", t], mixT_hi[:, 0:4, t * P:(t + 1) * P],
                            bank1["gateT", t])
            qkT_hi(6)
            proj_drain(16)
            qkT_hi(7)

            def softmax(unit):
                n = (unit // PAIRS + 1) * P
                act.wait_ge(max_ready, unit + 1)
                for s in range(2):
                    last = nc.scalar.activation(probs[:, unit % 2, s, 0:n], psum[:, BANK_S + s, 0:n],
                                                ACT.Exp, bias=neg_max[:, s:s + 1], scale=SCALE,
                                                accum_out=rowsum[:, unit, s:s + 1])
                last.then_inc(probs_ready, 1)

            def drain_pt1(unit):
                n = (unit // PAIRS + 1) * P
                act.wait_ge(pt_filled, 2 * unit + 2)
                nc.scalar.activation(probsT[:, 1].rearrange("p k q -> p (k q)")[:, 0:n],
                                     psum[:, BANK_PT + 1, 0:n], ACT.Copy).then_inc(pt1_drained, 1)

            def square_attn(qt):
                act.wait_ge(attn_ready, qt + 1)
                square(attn[:], ss_at[:, qt:qt + 1], at_squared)

            def attn_turn_hi(qt):
                turn_hi(filled1["attnT", qt], mixT_hi[:, 4:8, qt * P:(qt + 1) * P], bank1["attnT", qt])

            def square_out(t):
                for half in range(HALVES):
                    n = 20 + 2 * t + half
                    act.wait_ge(filled, filled1["proj", n])
                    square(psum[:, bank1["proj", n], :], ss_o[:, 2 * t + half:2 * t + half + 1], o_squared)

            def square_h1(t):
                act.wait_ge(*drained["proj", 21 + 2 * t])
                square(h[:, t, :], ss_h[:, t:t + 1], h1_squared)

            def norm_h1(t):
                act.wait_ge(h1_rstd, t + 1)
                if t == 0:
                    act.wait_ge(filled, filled1["qkT", 7])
                else:
                    act.wait_ge(filled, filled1["hT", 2 * t - 1])
                nc.scalar.activation(work[:].rearrange("p a n -> p (a n)"), h[:, t, :], ACT.Copy,
                                     scale=rstd_h[:, t:t + 1]).then_inc(hn_ready, 1)

            def hn_turn_hi(i):
                t, j = divmod(i, 2)
                turn_hi(filled1["hT", i], actT_hi[:, 4 * j:4 * j + 4, t * P:(t + 1) * P], bank1["hT", i])

            for step in range(TT * PAIRS):
                if step >= 6 and step % 4 == 2:
                    attn_turn_hi(step // 4 - 1)
                if step >= 1:
                    drain_pt1(step - 1)
                softmax(step)
                for slab in STEP_SPLITS.get(step, ()):
                    splits(slab)
                if step in (1, 3, 5):
                    proj_drain(17 + step // 2)
                if step == 10:
                    square_out(0)
                if step == 12:
                    square_h1(0)
                    norm_h1(0)
                if step >= 4 and step % 4 == 0:
                    square_attn(step // 4 - 1)
                if step == 14:
                    square_out(1)
            drain_pt1(15)
            square_h1(1)
            hn_turn_hi(0)
            hn_turn_hi(1)
            norm_h1(1)
            square_attn(3)
            act.wait_ge(pv_done, 16)
            act.dma_start(pT_raw[:], pT).then_inc(pT_loaded, 16)
            hn_turn_hi(2)
            hn_turn_hi(3)
            attn_turn_hi(3)
            square_out(2)
            for i in range(2):
                splits(SLAB_PLE + 2 * i)
            act.wait_ge(pT_loaded, 16)
            nc.scalar.activation(pT_hi[:], pT_raw[:], ACT.Copy).then_inc(pT_hi_done, 1)
            square_h1(2)
            split_hi_pair(SLAB_FF, G_O1 * KD - 2)
            norm_h1(2)
            square_out(3)
            split_hi_pair(SLAB_FF + 2, G_O1 * KD)
            hn_turn_hi(4)
            hn_turn_hi(5)
            square_h1(3)
            split_hi_pair(SLAB_FF + 4, G_O1 * KD + 6)
            norm_h1(3)
            hn_turn_hi(6)
            hn_turn_hi(7)
            split_hi_pair(SLAB_FF + 6, G_O1 * KD + 8)
            act.wait_ge(*drained["proj", 27])
            act.dma_start(gain_post[:], rows["mlp_post"]).then_inc(post_loaded, 16)
            act.wait_ge(slab_used, SLAB_FF)

            def mlp_tiles(c, tiles, gate_next=False):
                for m in tiles:
                    i, j = divmod(m, TT)
                    off = KD * (i + 1) + 2 * j
                    s = SLAB_FF + off
                    act.wait_ge(raw_loaded[s // 2 % 2],
                                16 * ((s // 2 - FIRST_PAIRS) // 2 + 1) + 16 * KD * c)
                    act.wait_ge(slab_used, s - 14 + SLABS_PER_CHUNK * c)
                    place_at = ((i + 1) % 2) * KD + 2 * j
                    gain = [mlp_pre(2 * j + a) if i in (0, 3) else None for a in range(2)]
                    if gate_next:
                        gain = [None, None]
                    split_hi(None, gain[0], raw[:, s % 4, :], place_at)
                    if m >= 8:
                        split_hi(None, gain[1], raw[:, (s + 1) % 4, :], place_at + 1)
                        continue
                    bank = psum[:, (m + 1) % 8, :]
                    relu = work[:, m % 2, :]
                    act.wait_ge(filled, FILLED_FF + m + 1 + 16 * c)
                    if m >= 2:
                        act.wait_ge(ff_squared, m - 1 + 8 * c)
                    nc.scalar.activation(relu, bank, ACT.Relu).then_inc(relu_done, 1)
                    split_hi(None, gain[1], raw[:, (s + 1) % 4, :], place_at + 1)
                    act.wait_ge(ff_squared, m + 1 + 8 * c)
                    nc.scalar.activation(mixT_hi[:, m, :], bank, ACT.Copy).then_inc(ff_hi_done, 1)

            with act.Fori(0, CHUNKS - 1) as c:
                mlp_tiles(c, range(16))
            last = CHUNKS - 1
            mlp_tiles(last, range(12))

            def square_down(t):
                act.wait_ge(*drained["down", t])
                square(acc[:, t, :], ss_dn[:, t:t + 1], dn_squared)

            def h2_turn_hi(i):
                t, j = divmod(i, 2)
                turn_hi(filled2["h2T", i], actT_hi[:, 4 * j:4 * j + 4, t * P:(t + 1) * P], bank2["h2T", i])

            def sigmoid(i):
                t, c0, width = GATE_TILES[i]
                act.wait_ge(*drained["gate", i])
                z = acc[:, t, c0:c0 + width]
                nc.scalar.activation(z, z, ACT.Sigmoid).then_inc(sig_done, 1)

            def square_ple(i):
                t, c0, width = GATE_TILES[i]
                act.wait_ge(pl_gated, i + 1)
                square(acc[:, t, c0:c0 + width], ss_pl[:, i:i + 1], pl_squared)

            mlp_tiles(last, (12, 13), gate_next=True)
            square_down(0)
            mlp_tiles(last, (14,), gate_next=True)
            square_down(1)
            mlp_tiles(last, (15,), gate_next=True)
            h2_turn_hi(0)
            h2_turn_hi(1)
            square_down(2)
            act.wait_ge(filled, filled2["down", 3])
            act.dma_start(gate_rows[:], rows["gate"]).then_inc(gate_rows_loaded, 16)
            h2_turn_hi(2)
            h2_turn_hi(3)
            square_down(3)
            splits(SLAB_GATE + KD)
            h2_turn_hi(4)
            h2_turn_hi(5)
            splits(SLAB_GATE + KD + 2)
            splits(SLAB_GATE + KD + 4)
            h2_turn_hi(6)
            h2_turn_hi(7)
            splits(SLAB_GATE + KD + 6)
            for i in range(len(GATE_TILES)):
                sigmoid(i)
                square_ple(i)

        @block.gpsimd
        def _(pool):
            done = [0]

            def after(instruction):
                done[0] += 1
                instruction.then_inc(pool_chain, 1)
                pool.wait_ge(pool_chain, done[0])

            nc.gpsimd.memset(minus_half, -0.5).then_inc(constants_set, 1)
            for matrix in (ident_bf, ident):
                after(nc.gpsimd.memset(matrix[:], 0.0))
                nc.gpsimd.affine_select(out=matrix[:], in_=matrix[:], compare_op=ALU.not_equal, fill=1.0,
                                        base=0, pattern=[[-1, P]], channel_multiplier=1
                                        ).then_inc(constants_set, 1)
            after(nc.gpsimd.memset(causal[:], 0.0))
            nc.gpsimd.affine_select(out=causal[:], in_=causal[:], compare_op=ALU.is_ge, fill=NEG,
                                    base=0, pattern=[[-1, P]], channel_multiplier=1
                                    ).then_inc(constants_set, 1)
            pool.wait_ge(constants_set, 4)

            def rstd(target, sums, n, ready, halves=None):
                width = target.shape[1]
                tmp = pool_tmp[:, 0:width]
                if halves is not None:
                    after(nc.gpsimd.tensor_tensor(tmp, sums, halves, ALU.add))
                    sums = tmp
                after(nc.gpsimd.tensor_scalar(tmp, sums, 1.0 / n, EPS, ALU.mult, ALU.add))
                nc.gpsimd.tensor_tensor(target, tmp, minus_half[:, 0:width], ALU.pow).then_inc(ready, 1)
                pool.wait_ge(ready, passed(ready))

            seen = {}

            def passed(ready):
                seen[id(ready)] = seen.get(id(ready), 0) + 1
                return seen[id(ready)]

            for t in range(TT):
                pool.wait_ge(x_squared, t + 1)
                rstd(rstd_x[:, t:t + 1], ss_x[:, t:t + 1], D, x_rstd)

            pool.wait_ge(ln_loaded, 16)
            for t in range(TT):
                pool.wait_ge(ln_mean, t + 1)
                rstd(rstd_ln[:, t:t + 1], mean_var[:, t, 1:2], 1, ln_rstd)
                pool.wait_ge(ln_centred, t + 1)
                after(nc.gpsimd.tensor_tensor(gv[:, t, :], gv[:, t, :], ln_gb[:, 0, :], ALU.mult))
                nc.gpsimd.tensor_tensor(gv[:, t, :], gv[:, t, :], ln_gb[:, 1, :], ALU.add
                                        ).then_inc(vn_ready, 1)

            pool.wait_ge(ws_loaded, 16)
            nc.gpsimd.affine_select(out=wsT[:], in_=wsT[:], compare_op=ALU.is_ge, fill=0.0, base=0,
                                    pattern=[[0, GROUPS], [1, P]], channel_multiplier=-1
                                    ).then_inc(ws_masked, 1)

            def rotate(i):
                t = i % TT
                rows_ = work[:, i % 2, :].rearrange("p (h d) -> p h d", d=DH)
                both, first, second = (rows_[:, :, 0:2 * HALF_ROPE], rows_[:, :, 0:HALF_ROPE],
                                       rows_[:, :, HALF_ROPE:2 * HALF_ROPE])
                cos = rope_sb[:, t:t + 1, 0, :].to_broadcast([P, HEADS, 2 * HALF_ROPE])
                sin = rope_sb[:, t:t + 1, 1, 0:HALF_ROPE].to_broadcast([P, HEADS, HALF_ROPE])
                pool.wait_ge(act_drained, 2 * TT + i + 1)
                nc.gpsimd.tensor_tensor(rope_tmp[:, 0], both, cos, ALU.mult)
                nc.gpsimd.tensor_tensor(rope_tmp[:, 1, :, HALF_ROPE:], first, sin, ALU.mult)
                after(nc.gpsimd.tensor_tensor(rope_tmp[:, 1, :, 0:HALF_ROPE], second, sin, ALU.mult))
                nc.gpsimd.tensor_tensor(first, rope_tmp[:, 0, :, 0:HALF_ROPE],
                                        rope_tmp[:, 1, :, 0:HALF_ROPE], ALU.subtract)
                nc.gpsimd.tensor_tensor(second, rope_tmp[:, 0, :, HALF_ROPE:],
                                        rope_tmp[:, 1, :, HALF_ROPE:], ALU.add).then_inc(roped, 1)
                pool.wait_ge(roped, i + 1)

            pool.wait_ge(rope_loaded, 16)
            for i in range(2 * TT):
                rotate(i)
                if i == 2:
                    pool.wait_ge(gm_squared, TT)
                    rstd(rstd_gm, ss_gm, W, gm_rstd)

            def attn_rstd(qt):
                pool.wait_ge(at_squared, qt + 1)
                rstd(rstd_at[:, qt:qt + 1], ss_at[:, qt:qt + 1], W, at_rstd)

            def out_rstd(t):
                pool.wait_ge(o_squared, 2 * t + 2)
                rstd(rstd_o[:, t:t + 1], ss_o[:, 2 * t:2 * t + 1], D, o_rstd,
                     ss_o[:, 2 * t + 1:2 * t + 2])

            def hidden_rstd(t):
                pool.wait_ge(h1_squared, t + 1)
                rstd(rstd_h[:, t:t + 1], ss_h[:, t:t + 1], D, h1_rstd)

            attn_rstd(0)
            attn_rstd(1)
            out_rstd(0)
            hidden_rstd(0)
            attn_rstd(2)
            out_rstd(1)
            hidden_rstd(1)
            attn_rstd(3)
            for t in (2, 3):
                out_rstd(t)
                hidden_rstd(t)
            pool.wait_ge(filled, filled1["ple", 7])
            nc.gpsimd.memset(acc[:], 0.0).then_inc(acc_zeroed, 1)
            for t in range(TT):
                pool.wait_ge(dn_squared, t + 1)
                rstd(rstd_dn[:, t:t + 1], ss_dn[:, t:t + 1], D, dn_rstd)
            for t in range(TT):
                *before, last_tile = gate_tiles_of(t)
                total = D * EPS
                for i in before:
                    partial = ple_tmp[:, i % 2:i % 2 + 1]
                    pool.wait_ge(pl_squared, i + 1)
                    after(nc.gpsimd.tensor_scalar(partial, ss_pl[:, i:i + 1], total, None, ALU.add))
                    total = partial
                pool.wait_ge(pl_squared, last_tile + 1)
                after(nc.gpsimd.tensor_scalar(ple_tmp[:, 2:3], ss_pl[:, last_tile:last_tile + 1], total,
                                              1.0 / D, ALU.add, ALU.mult))
                nc.gpsimd.tensor_tensor(rstd_pl[:, t:t + 1], ple_tmp[:, 2:3], minus_half[:, 0:1], ALU.pow
                                        ).then_inc(pl_rstd, 1)
                pool.wait_ge(pl_rstd, t + 1)

        @block.sync
        def _(sp):
            for item in FIRST_ORDER:
                if isinstance(item, str):
                    i = int(item[1])
                    t, ks = X_PIECES[i]
                    part = slice(ks[0], ks[-1] + 1)
                    sp.dma_start(xT_raw[:, t, part], xT[t][:, part]).then_inc(xT_loaded[i], 16)
                else:
                    sp.dma_start(raw_place(item), weights[item // 2][:, item % 2, :]
                                 ).then_inc(first_loaded[item], 16)
            for j in range(2):
                sp.dma_start(h[:, j, :], x[j * P:(j + 1) * P]).then_inc(x_loaded[j], 16)
                sp.dma_start(raw[:, 2 * j:2 * j + 2, :], weights[FIRST_PAIRS + j]).then_inc(raw_loaded[j], 16)
            turns = weights.rearrange("(i j) p k n -> i j p k n", j=2)
            with sp.Fori(FIRST_PAIRS // 2 + 1, PAIRS_OF_SLABS // 2) as i:
                for j in range(2):
                    sp.wait_ge(slab_lo, 4 * i + 2 * j - 2)
                    sp.dma_start(raw[:, 2 * j:2 * j + 2, :],
                                 turns[bass.ds(i, 1), j].rearrange("a p k n -> p (a k) n")
                                 ).then_inc(raw_loaded[j], 16)
            order = [i for t in range(TT) for i in gate_tiles_of(t)]
            for n, i in enumerate(order):
                t, c0, width = GATE_TILES[i]
                sp.wait_ge(out_ready, n + 1)
                sp.dma_start(out[t * P:(t + 1) * P, c0:c0 + width], h[:, t, c0:c0 + width]
                             ).then_inc(stored, 16)
            sp.wait_ge(stored, 16 * len(order))

        @block.tensor
        def _(pe):
            last_use_pending = [False]

            def product(out, a_hi, a_lo, b_hi, b_lo, first, last):
                begin = nc.tensor.matmul(out, a_hi, b_hi, start=first, stop=False)
                if last_use_pending[0]:
                    begin.then_inc(slab_used, 1)
                    last_use_pending[0] = False
                nc.tensor.matmul(out, a_hi, b_lo, start=False, stop=False)
                return nc.tensor.matmul(out, a_lo, b_hi, start=False, stop=last)

            def bank_free(names, banks, name):
                i = names.index(name)
                users = [n for n in names[:i] if banks[n] == banks[name]]
                if users:
                    pe.wait_ge(*drained[users[-1]])

            def rows_tile(out, k_range, act_hi, act_lo, t, slab, parts, slab_arrives, last_use,
                          columns=slice(0, W)):
                cut = slice(t * P, (t + 1) * P)
                for k in k_range:
                    if slab_arrives:
                        pe.wait_ge(slab_lo, slab + k + 1)
                    w = ring(slab + k)
                    mm = product(out, act_hi[:, k, cut], act_lo[:, k, cut], w_hi[:, w, columns],
                                 w_lo[:, w, columns], k == 0, k == parts - 1)
                    last_use_pending[0] = last_use
                    if k == parts - 1:
                        mm.then_inc(filled, 1)

            def proj(n, k_range=range(KD)):
                name = ("proj", n)
                if k_range[0] == 0:
                    bank_free(phase1, bank1, name)
                out = psum[:, bank1[name], :]
                if n < 20:
                    group, t = divmod(n, TT)
                    for k in k_range:
                        if n < TT:
                            for i, (tile, ks) in enumerate(X_PIECES):
                                if tile == t and ks[0] == k:
                                    pe.wait_ge(xT_lo_done, i + 1)
                        rows_tile(out, (k,), actT_hi, actT_lo, t, group * KD, KD, t == 0, t == TT - 1)
                    return
                t, half = divmod(n - 20, HALVES)
                if t == 0 and half == 0 and k_range[0] == 0:
                    pe.wait_ge(*drained["gateT", TT - 1])
                if half == 0 and k_range[-1] == KD - 1:
                    pe.wait_ge(*drained["attnT", t])
                rows_tile(out, k_range, mixT_hi, mixT_lo, t, (G_O0 + half) * KD, KD, t == 0, t == TT - 1)

            def turn(names, banks, name, source):
                bank_free(names, banks, name)
                for j in range(4):
                    mm = nc.tensor.transpose(psum[:, banks[name], j * P:(j + 1) * P],
                                             source[:, j * P:(j + 1) * P], ident[:])
                mm.then_inc(filled, 1)

            def mix(i):
                name = ("mix", i)
                bank_free(phase1, bank1, name)
                if i == 0:
                    pe.wait_ge(ws_masked, 1)
                    pe.wait_ge(vn_ready, TT)
                for a in range(2):
                    g = 2 * i + a
                    out = psum[:, bank1[name], a * 256:(a + 1) * 256].rearrange("p (t d) -> p t d", d=GD)
                    mm = nc.tensor.matmul(out, wsT[:, g, :], gv[:, :, g * GD:(g + 1) * GD],
                                          start=True, stop=True)
                mm.then_inc(filled, 1)

            def turn_qk(i):
                pe.wait_ge(roped, i + 1)
                turn(phase1, bank1, ("qkT", i), work[:, i % 2, :])

            def turn_gate(t):
                pe.wait_ge(gm_scaled, t + 1)
                turn(phase1, bank1, ("gateT", t), u[:, t, :])

            def turn_hn(i):
                t, j = divmod(i, 2)
                pe.wait_ge(hn_ready, t + 1)
                turn(phase1, bank1, ("hT", i), work[:, j, :])

            def turn_attn(qt):
                pe.wait_ge(at_scaled, qt + 1)
                turn(phase1, bank1, ("attnT", qt), attn[:])

            pe.wait_ge(constants_set, 2)
            for _ in range(WARM_UP_MATMULS):
                nc.tensor.matmul(psum[:, BANK_O, 0:P], ident_bf[:], ident_bf[:], start=True, stop=True)
            for part in (range(0, 3), range(3, KD)):
                proj(0, part)
                proj(1, part)
            pe.wait_ge(constants_set, 4)
            for n in range(2, 17):
                if n - 1 in (8, 9):
                    mix(2 * (n - 9))
                    mix(2 * (n - 9) + 1)
                if n - 1 >= 9:
                    turn_qk(n - 10)
                if 12 <= n - 1 <= 15:
                    turn_gate(n - 13)
                proj(n)
            turn_qk(7)

            def scores(unit):
                qt, pair = divmod(unit, PAIRS)
                n = (qt + 1) * P
                if unit == 0:
                    pe.wait_ge(*drained["mix", 3])
                if pair == 0:
                    pe.wait_ge(*drained["qkT", TT + qt])
                if unit >= 1:
                    pe.wait_ge(probs_ready, unit)
                for s in range(2):
                    part = slice(s * DH, (s + 1) * DH)
                    mm = product(psum[:, BANK_S + s, 0:n],
                                 qT_hi[part, pair, qt * P:n], qT_lo[part, pair, qt * P:n],
                                 kT_hi[part, pair, 0:n], kT_lo[part, pair, 0:n], True, True)
                mm.then_inc(scores_ready, 1)

            def turn_probs(unit):
                qt = unit // PAIRS
                pe.wait_ge(probs_ready, unit + 1)
                if unit == 0:
                    pe.wait_ge(*drained["qkT", 2 * TT - 1])
                for s in range(2):
                    for k in range(qt + 1):
                        mm = nc.tensor.transpose(psum[:, BANK_PT + s, k * P:(k + 1) * P],
                                                 probs[:, unit % 2, s, k * P:(k + 1) * P], ident[:])
                    mm.then_inc(pt_filled, 1)

            def attend(unit):
                qt, pair = divmod(unit, PAIRS)
                if unit == 0:
                    pe.wait_ge(*drained["gateT", TT - 1])
                if pair == 0:
                    pe.wait_ge(act_drained, 16 + qt + 1)
                    if qt:
                        pe.wait_ge(attn_ready, qt)
                for s in range(2):
                    head = 2 * pair + s
                    pe.wait_ge((pt0_drained, pt1_drained)[s], unit + 1)
                    for k in range(qt + 1):
                        mm = nc.tensor.matmul(psum[:, BANK_O, head * DH:(head + 1) * DH],
                                              probsT[:, s, k, :], v[:, k, head * DH:(head + 1) * DH],
                                              start=(k == 0), stop=(k == qt))
                mm.then_inc(pv_done, 1)

            for step in range(TT * PAIRS):
                scores(step)
                if step >= 1:
                    turn_probs(step - 1)
                n, k0 = STEP_TILES[step]
                proj(n, range(k0, k0 + 4))
                if step >= 1:
                    attend(step - 1)
                if step in (5, 9, 13):
                    turn_attn(step // 4 - 1)
            turn_probs(15)
            proj(25, range(0, 4))
            pe.wait_ge(pt0_drained, TT * PAIRS)
            pe.wait_ge(pt1_drained, TT * PAIRS)
            turn_hn(0)
            turn_hn(1)
            attend(15)
            proj(25, range(4, 8))
            turn_hn(2)
            turn_hn(3)
            turn_attn(3)
            for part in (range(0, 4), range(4, KD)):
                proj(26, part)
                proj(27, part)

            def ple_tile(i):
                half, t = divmod(i, TT)
                name = ("ple", i)
                bank_free(phase1, bank1, name)
                if i == 0:
                    pe.wait_ge(pT_lo_done, 1)
                rows_tile(psum[:, bank1[name], :], range(KP), pT_hi, pT_lo, t, SLAB_PLE + half * KP, KP,
                          t == 0, t == TT - 1)

            for i in range(3):
                ple_tile(i)
            turn_hn(4)
            turn_hn(5)
            for i in range(3, 6):
                ple_tile(i)
            turn_hn(6)
            turn_hn(7)
            ple_tile(6)
            ple_tile(7)
            before_mlp = drained["before_mlp"][1]
            pe.wait_ge(*drained["hT", 7])
            pe.wait_ge(*drained[[name for name in phase1 if bank1[name] == 1][-1]])

            def mlp_tiles(c, tiles):
                for m in tiles:
                    i, j = divmod(m, TT)
                    out = psum[:, (m + 1) % 8, :]
                    if m != 0:
                        pe.wait_ge(dve_drained, before_mlp + max(m - 7, 0) + 16 * c)
                    for k in range(KD):
                        if j == 0:
                            pe.wait_ge(slab_lo, SLAB_FF + KD * i + k + 1 + SLABS_PER_CHUNK * c)
                        if m == 8:
                            pe.wait_ge(dve_drained, before_mlp + k + 1 + 16 * c)
                        w = i % 2 * KD + k
                        cut = slice(j * P, (j + 1) * P)
                        if m < 8:
                            mm = product(out, w_hi[:, w, cut], w_lo[:, w, cut], actT_hi[:, k, :],
                                         actT_lo[:, k, :], k == 0, k == KD - 1)
                        else:
                            mm = product(out, mixT_hi[:, k, cut], mixT_lo[:, k, cut], w_hi[:, w, :],
                                         w_lo[:, w, :], k == 0, k == KD - 1)
                        last_use_pending[0] = j == TT - 1
                    mm.then_inc(filled, 1)

            with pe.Fori(0, CHUNKS - 1) as c:
                mlp_tiles(c, range(16))
            last = CHUNKS - 1
            mlp_tiles(last, range(15))

            def turn_h2(i):
                t, j = divmod(i, 2)
                pe.wait_ge(h2_ready, t + 1)
                turn(tail, bank2, ("h2T", i), h[:, t, j * W:(j + 1) * W])

            def gate_tile(i):
                t, c0, width = GATE_TILES[i]
                half, first = divmod(c0, W)
                bank_free(tail, bank2, ("gate", i))
                if c0 == 0:
                    pe.wait_ge(*drained["h2T", 2 * t + 1])
                rows_tile(psum[:, bank2["gate", i], 0:width], range(KD), actT_hi, actT_lo, t,
                          SLAB_GATE + half * KD, KD, t == 0, False, slice(first, first + width))

            turn_h2(0)
            turn_h2(1)
            mlp_tiles(last, (15,))
            turn_h2(2)
            turn_h2(3)
            gate_tile(0)
            turn_h2(4)
            turn_h2(5)
            gate_tile(1)
            turn_h2(6)
            turn_h2(7)
            for i in range(2, len(GATE_TILES)):
                gate_tile(i)


def slab_pairs(w):
    rows, columns = w.shape
    w = w.reshape(rows // 256, 2, P, columns // W, W).transpose(3, 0, 2, 1, 4)
    return w.reshape(-1, P, 2, W)


def kernel(**inputs):
    import numpy as _np
    import concourse.bacc as _bacc
    from concourse import mybir as _mybir
    from concourse.bass_utils import run_bass_kernel_spmd as _run

    a = {name: _np.asarray(value)[0] for name, value in inputs.items()}
    w_in, w_o, w_up, w_down = a["w_in"], a["w_o"], a["w_up"], a["w_down"]
    piece = [w_in[:, i * W:(i + 1) * W] for i in range(5)]
    stream = [slab_pairs(piece[i]) for i in (4, 3, 0, 1, 2)]
    stream.append(slab_pairs(_np.concatenate([w_o[W:], w_o[:W]])))
    stream.append(slab_pairs(a["w_ple"]))
    for c in range(CHUNKS):
        stream += [slab_pairs(w_up[:, c * D:(c + 1) * D]), slab_pairs(w_down[c * D:(c + 1) * D])]
    stream.append(slab_pairs(a["w_ple_gate"]))
    x = a["x"]
    angle_rate = _np.float32(500000.0) ** (-_np.arange(HALF_ROPE, dtype=_np.float32) / _np.float32(HALF_ROPE))
    angle = _np.arange(SEQ, dtype=_np.float32)[:, None] * angle_rate[None, :].astype(_np.float32)
    cos, sin = _np.cos(angle), _np.sin(angle)
    rope = _np.stack([_np.concatenate([cos, cos], 1), _np.concatenate([sin, sin], 1)], 1)
    as_columns = lambda g: g.reshape(-1, P).T
    arrays = {
        "x": x,
        "xT": x.reshape(TT, P, KD, P).transpose(0, 3, 2, 1),
        "pT": a["p"][0].reshape(SEQ, KP, P).transpose(2, 1, 0),
        "weights": _np.concatenate(stream),
        "columns": _np.concatenate([as_columns(a["mix_pre_g"]), as_columns(a["mlp_pre_g"]),
                                    as_columns(a["gmlp_out_g"]), as_columns(a["attn_out_g"]),
                                    a["b_s"].T], 1),
        "rope": rope.reshape(TT, P, 2, 2 * HALF_ROPE).transpose(1, 0, 2, 3).astype(_np.float32),
        "ws": a["w_s"].transpose(2, 0, 1),
        "row_ln": _np.stack([a["gmlp_ln_g"], a["gmlp_ln_b"]])[None],
        "row_mix_post": a["mix_post_g"][None],
        "row_mlp_post": a["mlp_post_g"][None],
        "row_gate": _np.stack([a["b_ple_gate"], a["ple_post_g"]])[None],
    }
    nc = _bacc.Bacc("TRN2", target_bir_lowering=False, num_devices=1)
    aps, fed = {}, {}
    for name, value in arrays.items():
        fed[name + "_dram"] = _np.ascontiguousarray(value)
        aps[name] = nc.dram_tensor(name + "_dram", value.shape, _mybir.dt.float32, kind="ExternalInput").ap()
    out = nc.dram_tensor("out_dram", (SEQ, D), _mybir.dt.float32, kind="ExternalOutput").ap()
    rows = {name[4:]: ap.to_broadcast([P, *ap.shape[1:]]) for name, ap in aps.items()
            if name.startswith("row_")}
    hymba_layer(nc, aps["x"], aps["xT"], aps["pT"], aps["weights"], aps["columns"], aps["rope"],
                aps["ws"], rows, out)
    result = _run(nc, [fed], core_ids=[0])
    return result.results[0]["out_dram"].reshape(1, SEQ, D)
```
